# Optimizing a Trainium2 kernel written in Bass

```python
import math
import jax, jax.numpy as jnp
from jax import lax
import numpy as np

D_MODEL = 1024
BATCH = 1
SEQ = 512
DEPTH = 2

CHUNK = 64
Q_BLOCK = 128
EPS = 1e-6

GLA_WIDTH = D_MODEL // 2
GLA_HEADS = 4
GLA_DK = GLA_WIDTH // 2 // GLA_HEADS
GLA_DV = GLA_WIDTH // GLA_HEADS
GLA_RANK = 16
GLA_TAU = 16.0

DIFF_WIDTH = D_MODEL - GLA_WIDTH
DIFF_HEADS = 4
DIFF_DH = DIFF_WIDTH // DIFF_HEADS // 2
DIFF_DV = 2 * DIFF_DH

D_FF = ((8 * D_MODEL // 3 + 127) // 128) * 128
CONV_W = 3

IN_SPLITS = (GLA_HEADS * GLA_DK, GLA_HEADS * GLA_DK, GLA_WIDTH, GLA_WIDTH, GLA_RANK,
             2 * DIFF_HEADS * DIFF_DH, 2 * DIFF_HEADS * DIFF_DH, DIFF_HEADS * DIFF_DV)
IN_COLS = sum(IN_SPLITS)

kernel_name = "hybrid_gla_diffattn_convffn_chunk_causal"

def rms_norm(x, g):
    xf = x.astype(jnp.float32)
    y = xf * lax.rsqrt(jnp.mean(xf * xf, axis=-1, keepdims=True) + EPS)
    return (y * g.astype(jnp.float32)).astype(x.dtype)

def split_cols(p):
    offs, acc = [], 0
    for s in IN_SPLITS[:-1]:
        acc += s
        offs.append(acc)
    return jnp.split(p, offs, axis=-1)

def gla_mixer(q, k, v, r, gate_low, w_gk_up, b_gk, norm_g):
    B, S, _ = q.shape
    N = S // CHUNK
    f32 = jnp.float32
    log_a = jax.nn.log_sigmoid((gate_low @ w_gk_up + b_gk).astype(f32)) / GLA_TAU

    def heads(t, d):
        return t.reshape(B, N, CHUNK, GLA_HEADS, d).transpose(0, 3, 1, 2, 4).astype(f32)

    qh = heads(q, GLA_DK) * (GLA_DK ** -0.5)
    kh = heads(k, GLA_DK)
    vh = heads(v, GLA_DV)
    la = heads(log_a, GLA_DK)
    cum = jnp.cumsum(la, axis=3)
    total = cum[:, :, :, -1:, :]
    k_dec = kh * jnp.exp(total - cum)
    q_dec = qh * jnp.exp(total)
    a_intra = jnp.einsum('bhncd,bhnsd->bhncs', qh, k_dec)
    o_intra = jnp.einsum('bhncs,bhnse->bhnce', a_intra, vh)
    chunk_kv = jnp.einsum('bhnsd,bhnse->bhnde', k_dec, vh)
    decay = jnp.exp(total[:, :, :, 0, :])

    def step(state, inp):
        d, kv = inp
        return d[..., None] * state + kv, state

    init = jnp.zeros((B, GLA_HEADS, GLA_DK, GLA_DV), f32)
    _, s_prev = lax.scan(step, init, (jnp.moveaxis(decay, 2, 0), jnp.moveaxis(chunk_kv, 2, 0)))
    s_prev = jnp.moveaxis(s_prev, 0, 2)
    o_inter = jnp.einsum('bhncd,bhnde->bhnce', q_dec, s_prev)
    o = (o_intra + o_inter).transpose(0, 2, 3, 1, 4).reshape(B, S, GLA_HEADS, GLA_DV)
    o = rms_norm(o, norm_g).reshape(B, S, GLA_WIDTH)
    return (o * jax.nn.silu(r.astype(f32))).astype(q.dtype)

def diff_mixer(q, k, v, q_norm_g, k_norm_g, lam_q1, lam_k1, lam_q2, lam_k2, sub_g, lambda_init):
    B, S, _ = q.shape
    f32 = jnp.float32
    NB = S // Q_BLOCK
    qh = rms_norm(q.reshape(B, S, DIFF_HEADS, 2, DIFF_DH).astype(f32), q_norm_g) * (DIFF_DH ** -0.5)
    kh = rms_norm(k.reshape(B, S, DIFF_HEADS, 2, DIFF_DH).astype(f32), k_norm_g)
    qh = qh.transpose(0, 2, 3, 1, 4)
    kh = kh.transpose(0, 2, 3, 1, 4)
    vh = v.reshape(B, S, DIFF_HEADS, DIFF_DV).transpose(0, 2, 1, 3).astype(f32)
    lam = (jnp.exp(jnp.sum(lam_q1.astype(f32) * lam_k1.astype(f32)))
           - jnp.exp(jnp.sum(lam_q2.astype(f32) * lam_k2.astype(f32))) + lambda_init)
    qb = qh.reshape(B, DIFF_HEADS, 2, NB, Q_BLOCK, DIFF_DH).transpose(3, 0, 1, 2, 4, 5)
    key_chunk = jnp.arange(S) // CHUNK

    def block(args):
        q_blk, i = args
        s = jnp.einsum('bhjqd,bhjkd->bhjqk', q_blk, kh)
        q_chunk = (i * Q_BLOCK + jnp.arange(Q_BLOCK)) // CHUNK
        mask = key_chunk[None, :] <= q_chunk[:, None]
        p = jax.nn.softmax(jnp.where(mask, s, -jnp.inf), axis=-1)
        a = p[:, :, 0] - lam * p[:, :, 1]
        return jnp.einsum('bhqk,bhke->bhqe', a, vh)

    o = lax.map(block, (qb, jnp.arange(NB)))
    o = o.transpose(1, 0, 3, 2, 4).reshape(B, S, DIFF_HEADS, DIFF_DV)
    o = rms_norm(o, sub_g) * (1.0 - lambda_init)
    return o.reshape(B, S, DIFF_WIDTH).astype(q.dtype)

def conv_ffn(h, w_up, conv_w, conv_b, w_down):
    u = h @ w_up
    C = u.shape[-1]
    u = lax.conv_general_dilated(u, conv_w[:, None, :], window_strides=(1,),
                                 padding=[(CONV_W - 1, 0)],
                                 dimension_numbers=('NWC', 'WIO', 'NWC'),
                                 feature_group_count=C) + conv_b
    gate, val = jnp.split(u, 2, axis=-1)
    return (jax.nn.silu(gate) * val) @ w_down

def setup_inputs(seed: int = 0) -> dict:
    key = jax.random.key(seed)
    ks = jax.random.split(key, 20)
    f32 = jnp.float32
    nrm = lambda k, shape, s: jax.random.normal(k, shape, f32) * s
    res_scale = (2 * DEPTH) ** -0.5
    return {
        "x": jax.random.normal(ks[0], (BATCH, SEQ, D_MODEL), f32),
        "norm1_g": 1.0 + nrm(ks[1], (DEPTH, D_MODEL), 0.02),
        "w_in": nrm(ks[2], (DEPTH, D_MODEL, IN_COLS), D_MODEL ** -0.5),
        "gla_w_gk_up": nrm(ks[3], (DEPTH, GLA_RANK, GLA_HEADS * GLA_DK), GLA_RANK ** -0.5),
        "gla_b_gk": nrm(ks[4], (DEPTH, GLA_HEADS * GLA_DK), 0.1),
        "gla_norm_g": 1.0 + nrm(ks[5], (DEPTH, GLA_DV), 0.02),
        "diff_q_norm_g": 1.0 + nrm(ks[6], (DEPTH, DIFF_DH), 0.02),
        "diff_k_norm_g": 1.0 + nrm(ks[7], (DEPTH, DIFF_DH), 0.02),
        "diff_lam_q1": nrm(ks[8], (DEPTH, DIFF_DH), 0.1),
        "diff_lam_k1": nrm(ks[9], (DEPTH, DIFF_DH), 0.1),
        "diff_lam_q2": nrm(ks[10], (DEPTH, DIFF_DH), 0.1),
        "diff_lam_k2": nrm(ks[11], (DEPTH, DIFF_DH), 0.1),
        "diff_sub_g": 1.0 + nrm(ks[12], (DEPTH, DIFF_DV), 0.02),
        "w_out": nrm(ks[13], (DEPTH, D_MODEL, D_MODEL), D_MODEL ** -0.5 * res_scale),
        "norm2_g": 1.0 + nrm(ks[14], (DEPTH, D_MODEL), 0.02),
        "ffn_w_up": nrm(ks[15], (DEPTH, D_MODEL, 2 * D_FF), D_MODEL ** -0.5),
        "ffn_conv_w": nrm(ks[16], (DEPTH, CONV_W, 2 * D_FF), CONV_W ** -0.5),
        "ffn_conv_b": nrm(ks[17], (DEPTH, 2 * D_FF), 0.02),
        "ffn_w_down": nrm(ks[18], (DEPTH, D_FF, D_MODEL), D_FF ** -0.5 * res_scale),
    }

def reference(x, norm1_g, w_in, gla_w_gk_up, gla_b_gk, gla_norm_g, diff_q_norm_g, diff_k_norm_g,
              diff_lam_q1, diff_lam_k1, diff_lam_q2, diff_lam_k2, diff_sub_g, w_out, norm2_g,
              ffn_w_up, ffn_conv_w, ffn_conv_b, ffn_w_down):
    for l in range(DEPTH):
        lambda_init = 0.8 - 0.6 * math.exp(-0.3 * l)
        h = rms_norm(x, norm1_g[l])
        g_q, g_k, g_v, g_r, g_low, d_q, d_k, d_v = split_cols(h @ w_in[l])
        o_gla = gla_mixer(g_q, g_k, g_v, g_r, g_low, gla_w_gk_up[l], gla_b_gk[l], gla_norm_g[l])
        o_diff = diff_mixer(d_q, d_k, d_v, diff_q_norm_g[l], diff_k_norm_g[l],
                            diff_lam_q1[l], diff_lam_k1[l], diff_lam_q2[l], diff_lam_k2[l],
                            diff_sub_g[l], lambda_init)
        x = x + jnp.concatenate([o_gla, o_diff], axis=-1) @ w_out[l]
        h2 = rms_norm(x, norm2_g[l])
        x = x + conv_ffn(h2, ffn_w_up[l], ffn_conv_w[l], ffn_conv_b[l], ffn_w_down[l])
    return x


_drawn_inputs = setup_inputs


def setup_inputs(seed=0):
    import zlib

    import numpy as np

    out = dict(_drawn_inputs(seed))
    spreads = {}
    factors = {'norm1_g': 3.041,
     'gla_b_gk': 4.268,
     'gla_norm_g': 8.0,
     'diff_q_norm_g': 7.536,
     'diff_k_norm_g': 7.431,
     'diff_lam_q1': 4.458,
     'diff_lam_q2': 3.177,
     'diff_lam_k2': 4.015,
     'diff_sub_g': 21.966,
     'norm2_g': 4.877,
     'ffn_conv_b': 4.993}
    for name, (base, spread) in spreads.items():
        noise = np.random.default_rng([zlib.crc32(name.encode()), seed]).standard_normal(out[name].shape)
        drawn = base * np.exp(spread * noise) if base else spread * noise
        out[name] = __import__('jax').numpy.asarray(drawn.astype(out[name].dtype))
    for name, factor in factors.items():
        out[name] = (out[name] * factor).astype(out[name].dtype)
    return out
```

```python
from contextlib import ExitStack

import concourse.bass as bass
import numpy as np
from concourse import mybir

F32 = mybir.dt.float32
F32R = mybir.dt.float32r
ALU = mybir.AluOpType
ACT = mybir.ActivationFunctionType
AX_X = mybir.AxisListType.X

P = 128
D = 1024
T = 512
L = 2
CHUNK = 64
EPS = 1e-6
KT = D // P
TT = T // P
NC = T // CHUNK
H = 4
DK = 64
DV = 128
DH = 64
RANK = 16
TAU = 16.0
FF = 2816
FT = FF // P
IN_SPLITS = (H * DK, H * DK, H * DV, H * DV, RANK, 2 * H * DH, 2 * H * DH, H * DV)
AHEAD = 3
RAW = 2
SLOTS = 4
DOWN_BLOCKS = (8, 8, 6)
NEG = -1.0e30

MIXER_UNITS = [("dv", 0), ("dv", 1), ("dv", 2), ("dv", 3), ("q", 0), ("k", 0), ("q", 1), ("k", 1),
               ("gk", 0), ("gk", 1), ("q", 2), ("k", 2), ("gv", 0), ("gv", 1), ("gv", 2), ("gv", 3),
               ("q", 3), ("k", 3), ("gq", 0), ("gq", 1), ("r", 0), ("r", 1), ("r", 2), ("r", 3)]
U_OUT = len(MIXER_UNITS)
U_UP = U_OUT + KT
U_DOWN = U_UP + 2 * FT
UNITS = U_DOWN + 3 * KT
assert UNITS % SLOTS == 0 and U_OUT % SLOTS == 0 and U_UP % SLOTS == 0 and U_DOWN % SLOTS == 0
UNIT_OF = {x: u for u, x in enumerate(MIXER_UNITS)}

PARTS = [[(0, 0), (1, 128)], [(2, 0)], [(3, 0)]]
STEPS = [(h, part) for h in range(H) for part in range(len(PARTS))]
SCORES_AT = [7, 8, 9, 10, 11, 12, 13, 14, 15, 19, 20, 21]
STEP_AT = {u: t for t, u in enumerate(SCORES_AT)}

SUMS = [("q0", 5), ("k0", 6), ("q1", 7), ("k1", 8), ("q2", 11), ("k2", 12), ("d0", 12), ("d1", 15),
        ("q3", 17), ("k3", 18), ("d2", 18), ("g0", 21), ("g1", 21), ("g2", 22), ("g3", 22), ("d3", 23)]
SUM_OF = {name: e for e, (name, _) in enumerate(SUMS)}
HEADS_LEAVE = [("d0", 11), ("d1", 14), ("d2", 17), ("g0", 20), ("g1", 20), ("g2", 21), ("g3", 21), ("d3", 23)]
OUT_ORDER = ["d0", "d1", "d2", "g0", "g1", "d3", "g2", "g3"]
OUT_TILE = {**{f"g{h}": h for h in range(H)}, **{f"d{h}": H + h for h in range(H)}}


def small_items(u):
    items = []
    if u == 0:
        items += [("ss", 0), ("rtok", 0)]
    if u - 1 in STEP_AT:
        items.append(("T", STEP_AT[u - 1]))
    if u == 9:
        items.append(("low", 0))
    if u == 10:
        items += [("z", 0), ("z", 1)]
    if u == 21:
        items += [("sum", SUM_OF["g0"]), ("sum", SUM_OF["g1"]), ("go", 2), ("go", 3)]
    else:
        items += [("sum", e) for e, (_, at) in enumerate(SUMS) if at == u]
    if u == 13:
        items += [("suf", 0), ("suf", 1)]
    if u == 14:
        items += [("dec", 0), ("dec", 1)]
    if 16 <= u < 20:
        items += [("kv", 2 * (u - 16)), ("kv", 2 * (u - 16) + 1)]
    if u == 20:
        items += [("go", 0), ("go", 1)]
    if u in STEP_AT:
        items.append(("scores", STEP_AT[u]))
    return items


def ring_of_banks():
    uses = []
    for u, (kind, n) in enumerate(MIXER_UNITS):
        if kind in ("dv", "gk", "gv"):
            if n % 2 == 0:
                uses += [(kind, n), (kind, n + 1)]
        else:
            uses.append((kind, n))
        uses += [x for x in small_items(u) if x[0] in ("low", "z", "sum", "suf", "dec", "kv", "go")]
    return uses + [("pad", n) for n in range(-len(uses) % 4)]


RING = ring_of_banks()
RING_AT = {x: n for n, x in enumerate(RING)}

C_N1 = 0
C_N2 = C_N1 + (L + 1) * KT
C_CONV = C_N2 + L * KT
C_GG = C_CONV + L * 4 * 2 * FT
C_SUB = C_GG + L
C_QG = C_SUB + L
C_KG = C_QG + L
C_LAMQ = C_KG + L
C_LAMK = C_LAMQ + 2 * L
N_PARAMS = C_LAMK + 2 * L
C_IDENT, C_BLOCKS, C_LATER = 0, P, 2 * P
C_HALVES = 3 * P
C_EPS = C_HALVES + 2
C_LAMINIT = C_EPS + 1
C_ONEMINUS = C_LAMINIT + L
N_CONSTS = C_ONEMINUS + L


def trunk(nc, x_in, units, low_in, gk_up_in, params_in, consts_in, out):
    with ExitStack() as ctx:
        base = nc.sbuf_base
        base += -base % 32
        at = [base]

        def place(name, shape, dt=F32, where=None):
            size = 4 * int(np.prod(shape[1:]))
            t = nc.alloc_sbuf_tensor_at(name, shape, dt, offset=at[0] if where is None else where)
            if where is None:
                at[0] += size + -size % 32
            return t

        x = place("x", [P, KT, T])
        h_hi = place("h_hi", [P, KT, T], F32R)
        h_lo = place("h_lo", [P, KT, T], F32R)
        raw = place("raw", [P, RAW, 1024])
        w_hi = place("w_hi", [P, SLOTS, 1024], F32R)
        w_lo = place("w_lo", [P, SLOTS, 1024], F32R)
        at_act_hi = at[0]
        act_hi = place("act_hi", [P, FT, T], F32R)
        at_act_lo = at[0]
        act_lo = place("act_lo", [P, FT, T], F32R)
        act_hi_f32 = place("act_hi_f32", [P, KT, T], F32, at_act_hi)
        act_lo_f32 = place("act_lo_f32", [P, KT, T], F32, at_act_lo)
        a0 = at_act_hi + 4 * KT * T
        vd = place("vd", [P, TT, T], F32, a0)
        vg = place("vg", [P, TT, T], F32, a0 + 8192)
        kg = place("kg", [P, 2, T], F32, a0 + 16384)
        gq = place("gq", [P, 2, T], F32, a0 + 20480)
        la = place("la", [P, 2, T], F32, a0 + 24576)
        b0 = at_act_lo + 4 * KT * T
        qk = place("qk", [P, 2 * H, T], F32, b0)
        state = place("state", [P, NC, 2, DV], F32, b0 + 16384)
        probs = place("probs", [P, 2, T], F32, b0 + 24576)
        at_c = at[0]
        u_buf = place("u_buf", [P, SLOTS, T + 2])
        c_buf = place("c_buf", [P, SLOTS, T])
        a_buf = place("a_buf", [P, 2, T], F32, at_c)
        aT = place("aT", [P, 2, T], F32, at_c + 4096)
        sq = place("sq", [P, 2, T], F32, at_c + 8192)
        rs = place("rs", [P, 2, T], F32, at_c + 12288)
        ones_buf = place("ones_buf", [P, P])
        rbc = place("rbc", [P, T])
        acc = place("acc", [P, T])
        sqx = place("sqx", [P, T])
        low_raw = place("low_raw", [P, L, KT * RANK])
        params = place("params", [P, N_PARAMS])
        consts = place("consts", [P, N_CONSTS])
        gk_up = place("gk_up", [RANK + 1, L, H * DK])
        rtok = place("rtok", [P, TT])
        neg_lam = place("neg_lam", [P, L])
        sub_g = place("sub_g", [P, L])
        lam_prod = place("lam_prod", [P, 2 * L])
        lam_exp = place("lam_exp", [P, 2 * L])
        lam_diff = place("lam_diff", [P, L])
        mx = place("mx", [P, 2, 4])
        neg_mx = place("neg_mx", [P, 2, 4])
        p_sum = place("p_sum", [P, 2, 4])
        p_rec = place("p_rec", [P, 2, 4])
        p_lam = place("p_lam", [P, 2, 2])
        decay = place("decay", [P, 2, NC])
        assert at[0] <= nc.sbuf_usable_end, (at[0], nc.sbuf_usable_end)
        low_hi = act_lo[:, 6, 0:KT * RANK]
        low_lo = act_lo[:, 7, 0:KT * RANK]
        gk_up_now = act_hi_f32[0:RANK + 1, 4, 0:H * DK]
        low_t = act_hi_f32[0:RANK + 1, 5, :]
        newton = act_lo_f32[:, 0:2, :]
        gate_tmp = act_hi_f32[:, 6:8, :]
        kd_tmp = act_hi_f32[:, 6:8, :]

        ident = consts[:, C_IDENT:C_IDENT + P]
        same_map = consts[:, C_BLOCKS:C_BLOCKS + P]
        later = consts[:, C_LATER:C_LATER + P]
        ones = ones_buf[:, :]
        halves = consts[:, C_HALVES:C_HALVES + 2]
        eps = consts[:, C_EPS:C_EPS + 1]
        one = ones_buf[:, 0:1]

        bank = [ctx.enter_context(nc.psum_tensor(f"bank{b}", [P, T], F32)) for b in range(4)]
        sc_ps = ctx.enter_context(nc.psum_tensor("sc_ps", [P, 2, T], F32))
        t_ps = ctx.enter_context(nc.psum_tensor("t_ps", [P, T], F32))
        o_ps = ctx.enter_context(nc.psum_tensor("o_ps", [P, T], F32))

        class Count:

            def __init__(self, name, each):
                self.sem, self.each = ctx.enter_context(nc.semaphore(name)), each

            def by(self, layer, k):
                return layer * self.each + k

        def sem(name):
            return ctx.enter_context(nc.semaphore(name))

        x_landed = [sem(f"x_landed{m}") for m in range(KT)]
        consts_landed, params_landed = sem("consts_landed"), sem("params_landed")
        raw_landed = [sem(f"raw_landed{s}") for s in range(RAW)]
        lam_prod_ready, lam_summed, lam_exp_ready = sem("lam_prod_ready"), sem("lam_summed"), sem("lam_exp_ready")
        lam_steps, ones_ready = sem("lam_steps"), sem("ones_ready")
        stored = sem("stored")
        hi_ready = Count("hi_ready", UNITS)
        lo_ready = Count("lo_ready", UNITS)
        unit_done = Count("unit_done", UNITS)
        x_ready = Count("x_ready", 2 * KT)
        h_hi_ready = Count("h_hi_ready", 2 * KT)
        h_lo_ready = Count("h_lo_ready", 2 * KT)
        sqx_ready = Count("sqx_ready", 2 * KT)
        acc_zeroed = Count("acc_zeroed", 2)
        acc_added = Count("acc_added", 2 * KT)
        tokens_summed = Count("tokens_summed", 3)
        ln_tokens = Count("ln_tokens", 3)
        r_ready = Count("r_ready", 3)
        layer_ready = Count("layer_ready", 4)
        v_ready = Count("v_ready", 2 * TT)
        gk_ready = Count("gk_ready", TT)
        gv_ready = Count("gv_ready", 2 * TT)
        qk_raw = Count("qk_raw", 2 * H)
        qk_ready = Count("qk_ready", 2 * H)
        gq_ready = Count("gq_ready", 2)
        rg_ready = Count("rg_ready", H)
        squared = Count("squared", len(SUMS))
        summed = Count("summed", len(SUMS))
        ln_done = Count("ln_done", len(SUMS))
        rs_ready = Count("rs_ready", len(SUMS))
        rs_squared = Count("rs_squared", 2 * H)
        newton_product = Count("newton_product", 2 * H)
        newton_factor = Count("newton_factor", 2 * H)
        qk_scaled = Count("qk_scaled", 2 * H)
        o_copied = Count("o_copied", 2 * H)
        o_normed = Count("o_normed", 2 * H)
        gated = Count("gated", H)
        silu_done = Count("silu_done", H)
        o_hi_ready = Count("o_hi_ready", 2 * H)
        o_lo_ready = Count("o_lo_ready", 2 * H)
        n_steps = len(STEPS)
        scores_done = Count("scores_done", n_steps)
        masked = Count("masked", n_steps)
        max_done = Count("max_done", n_steps)
        neg_max_ready = Count("neg_max_ready", n_steps)
        probs_ready = Count("probs_ready", n_steps)
        rec_ready = Count("rec_ready", n_steps)
        lam_scaled = Count("lam_scaled", n_steps)
        a_half = Count("a_half", n_steps)
        a_ready = Count("a_ready", n_steps)
        transposed = Count("transposed", n_steps)
        aT_ready = Count("aT_ready", n_steps)
        pv_done = Count("pv_done", n_steps)
        low_done = Count("low_done", 1)
        low_ready = Count("low_ready", 1)
        z_done = Count("z_done", 2)
        z_abs = Count("z_abs", 2)
        z_exp = Count("z_exp", 2)
        z_log = Count("z_log", 2)
        la_ready = Count("la_ready", 2)
        suffix_done = Count("suffix_done", 2)
        kd_ready = Count("kd_ready", 2)
        k_decayed = Count("k_decayed", 2)
        decay_done = Count("decay_done", 2)
        decay_ready = Count("decay_ready", 2)
        kv_done = Count("kv_done", NC)
        state_ready = Count("state_ready", NC)
        go_done = Count("go_done", H)
        pads_zeroed = Count("pads_zeroed", 1)
        u_ready = Count("u_ready", 2 * FT)
        tap2_done = Count("tap2_done", 2 * FT)
        tap1_done = Count("tap1_done", 2 * FT)
        conv_done = Count("conv_done", 2 * FT)
        gate_ready = Count("gate_ready", FT)
        product_ready = Count("product_ready", FT)
        act_hi_ready = Count("act_hi_ready", FT)
        act_lo_ready = Count("act_lo_ready", FT)

        qk_sums = [e for e, (name, _) in enumerate(SUMS) if name[0] in "qk"]
        o_sums = [e for e, (name, _) in enumerate(SUMS) if name[0] in "dg"]

        FREED = {}
        for kind, n in RING:
            if kind == "pad":
                FREED[kind, n] = FREED[RING[RING_AT[kind, n] - 4]]
                continue
            FREED[kind, n] = {
                "dv": lambda n: (v_ready, TT * (n // 2) + 2 * (n % 2) + 2), "gk": lambda n: (gk_ready, 2 * n + 2),
                "gv": lambda n: (gv_ready, TT * (n // 2) + 2 * (n % 2) + 2),
                "q": lambda n: (qk_raw, 2 * n + 1), "k": lambda n: (qk_raw, 2 * n + 2),
                "gq": lambda n: (gq_ready, n + 1), "r": lambda n: (rg_ready, n + 1),
                "low": lambda n: (low_ready, 1),
                "z": lambda n: (la_ready, n + 1), "suf": lambda n: (kd_ready, n + 1),
                "dec": lambda n: (decay_ready, n + 1), "kv": lambda n: (state_ready, n + 1),
                "sum": lambda n: (newton_product, qk_sums.index(n) + 1) if n in qk_sums else (ln_done, n + 1),
                "go": lambda n: (squared, SUM_OF[f"g{n}"] + 1),
            }[kind](n)

        RS_USED = {**{e: (qk_ready, k + 1) for k, e in enumerate(qk_sums)},
                   **{e: (o_normed, k + 1) for k, e in enumerate(o_sums)}}
        def freed(n):
            return (h_lo_ready, 4 + n + 1) if n < 4 else FREED[RING[n - 4]]

        def take_bank(layer, use):
            n = RING_AT[use]
            last_use, k = freed(n)
            nc.tensor.wait_ge(last_use.sem, last_use.by(layer, k))
            return bank[n % 4]

        def take_two(layer, use):
            n = RING_AT[use]
            (a, k), (b, j) = freed(n), freed(n + 1)
            if a is not b:
                nc.tensor.wait_ge(a.sem, a.by(layer, k))
            nc.tensor.wait_ge(b.sem, b.by(layer, j))

        def bank_of(use):
            return bank[RING_AT[use] % 4]

        def head_slot(name):
            return OUT_TILE[name]

        block = ctx.enter_context(nc.Block())

        @block.sync
        def _(sp):
            def load(n, s):
                sp.dma_start(raw[:, s, :], units[n]).then_inc(raw_landed[s], 16)

            sp.dma_start(params[:, :], params_in).then_inc(params_landed, 16)
            sp.dma_start(x[:, 0, :], x_in[0]).then_inc(x_landed[0], 16)
            load(0, 0)
            for m in range(1, KT // 2):
                sp.dma_start(x[:, m, :], x_in[m]).then_inc(x_landed[m], 16)
            load(1, 1)
            for m in range(KT // 2, KT):
                sp.dma_start(x[:, m, :], x_in[m]).then_inc(x_landed[m], 16)
            with sp.Fori(1, L * UNITS // RAW + 1) as i:
                for s in range(RAW):
                    sp.wait_ge(lo_ready.sem, (i - 1) * RAW + s + 1)
                    load(i * RAW + s, s)
            last = L * UNITS + RAW
            for n in range(last, L * UNITS + AHEAD):
                sp.wait_ge(lo_ready.sem, n - RAW + 1)
                load(n, n % RAW)
            for s in range(RAW):
                sp.wait_ge(raw_landed[s], 16 * len(range(s, L * UNITS + AHEAD, RAW)))

        @block.gpsimd
        def _(pool):
            def split_lo(layer, u0, s):
                slot = s % SLOTS
                pool.wait_ge(hi_ready.sem, hi_ready.by(layer, u0 + s + 1))
                nc.gpsimd.tensor_tensor(w_lo[:, slot, :], raw[:, slot % RAW, :], w_hi[:, slot, :].bitcast(F32),
                                        ALU.subtract).then_inc(lo_ready.sem, 1)

            def add_square(layer, k, zeroed):
                pool.wait_ge(sqx_ready.sem, sqx_ready.by(layer, k + 1))
                pool.wait_ge(acc_zeroed.sem, acc_zeroed.by(layer, zeroed))
                pool.wait_ge(acc_added.sem, acc_added.by(layer, k))
                nc.gpsimd.tensor_tensor(acc[:, :], acc[:, :], sqx[:, :], ALU.add).then_inc(acc_added.sem, 1)

            for n in range(AHEAD):
                split_lo(0, 0, n)
            with pool.Fori(0, L) as layer:
                with pool.Fori(0, U_OUT // SLOTS) as i:
                    for s in range(SLOTS):
                        split_lo(layer, i * SLOTS, s + AHEAD)
                with pool.Fori(0, KT // SLOTS) as i:
                    for s in range(SLOTS):
                        split_lo(layer, i * SLOTS + U_OUT, s + AHEAD)
                        add_square(layer, i * SLOTS + KT + s, 2)
                with pool.Fori(0, 2 * FT // SLOTS) as i:
                    for s in range(SLOTS):
                        split_lo(layer, i * SLOTS + U_UP, s + AHEAD)
                with pool.Fori(0, KT // SLOTS) as i:
                    for s in range(SLOTS):
                        for j in range(3):
                            split_lo(layer, i * 3 * SLOTS + U_DOWN, 3 * s + j + AHEAD)
                        add_square(layer, i * SLOTS + 2 * KT + s, 3)

        @block.scalar
        def _(act):
            def activate(*args, **kw):
                return nc.scalar.activation(*args, **kw)

            def split_hi(layer, u0, s):
                slot = s % SLOTS
                act.wait_ge(raw_landed[slot % RAW],
                            layer * (UNITS // RAW * 16) + u0 * (16 // RAW) + (s // RAW + 1) * 16)
                if not (isinstance(layer, int) and layer * UNITS + u0 + s < SLOTS):
                    act.wait_ge(unit_done.sem, unit_done.by(layer, u0 + (s - SLOTS + 1)))
                activate(w_hi[:, slot, :], raw[:, slot % RAW, :], ACT.Copy).then_inc(hi_ready.sem, 1)

            def normed_tile(layer, k, m, g_col):
                act.wait_ge(acc_added.sem, acc_added.by(layer, k))
                activate(h_hi[:, m, :], x[:, m, :], ACT.Copy, scale=params[:, bass.ds(g_col, 1)]).then_inc(h_hi_ready.sem, 1)
                activate(sqx[:, :], x[:, m, :], ACT.Square).then_inc(sqx_ready.sem, 1)

            def rsqrt_mean(layer, which, dst, src, width):
                act.wait_ge(tokens_summed.sem, tokens_summed.by(layer, which + 1))
                activate(dst, src, ACT.Ln, scale=1.0 / width, bias=eps).then_inc(ln_tokens.sem, 1)
                act.wait_ge(ln_tokens.sem, ln_tokens.by(layer, which + 1))
                activate(dst, dst, ACT.Exp, scale=-0.5).then_inc(r_ready.sem, 1)

            def exp_and_ln():
                nc.scalar.preload_act_table_set("natural_log_exp_and_others")

            exp_and_ln()
            act.wait_ge(params_landed, 16)
            for m in range(KT):
                act.wait_ge(x_landed[m], 16)
                normed_tile(0, m, m, C_N1 + m)
                if m in (0, 3):
                    split_hi(0, 0, m // 3)
                if m == 1:
                    for dst, src in ((consts[:, :], consts_in), (low_raw[:, :, :], low_in), (gk_up[:, :, :], gk_up_in)):
                        act.dma_start(dst, src).then_inc(consts_landed, 16)
            split_hi(0, 0, 2)
            act.wait_ge(consts_landed, 48)
            act.wait_ge(lam_summed, 1)
            activate(lam_exp[:, :], t_ps[:, 0:2 * L], ACT.Exp).then_inc(lam_exp_ready, 1)

            def square_qk(layer, name):
                e = SUM_OF[name]
                j = 2 * int(name[1]) + (name[0] == "k")
                act.wait_ge(qk_raw.sem, qk_raw.by(layer, j + 1))
                if e >= 2:
                    act.wait_ge(summed.sem, summed.by(layer, e - 1))
                activate(sq[:, e % 2, :], qk[:, j, :], ACT.Square).then_inc(squared.sem, 1)

            def copy_and_square_head(layer, name):
                e, h = SUM_OF[name], int(name[1])
                if name[0] == "d":
                    act.wait_ge(pv_done.sem, pv_done.by(layer, len(PARTS) * (h + 1)))
                    src, dst, scale = o_ps, act_lo_f32[:, head_slot(name), :], 1.0
                else:
                    act.wait_ge(go_done.sem, go_done.by(layer, h + 1))
                    src, dst, scale = bank_of(("go", h)), act_hi_f32[:, head_slot(name), :], DK ** -0.5
                activate(dst, src[:, :], ACT.Copy, scale=scale).then_inc(o_copied.sem, 1)
                if e >= 2:
                    act.wait_ge(summed.sem, summed.by(layer, e - 1))
                activate(sq[:, e % 2, :], src[:, :], ACT.Square, scale=scale).then_inc(squared.sem, 1)

            def rsqrt_sum(layer, e):
                name = SUMS[e][0]
                width = DH if name[0] in "qk" else DV
                act.wait_ge(summed.sem, summed.by(layer, e + 1))
                if e >= 2:
                    last_use, k = RS_USED[e - 2]
                    act.wait_ge(last_use.sem, last_use.by(layer, k))
                activate(rs[:, e % 2, :], bank_of(("sum", e))[:, :], ACT.Ln, scale=1.0 / width, bias=eps)\
                    .then_inc(ln_done.sem, 1)
                act.wait_ge(ln_done.sem, ln_done.by(layer, e + 1))
                activate(rs[:, e % 2, :], rs[:, e % 2, :], ACT.Exp, scale=-0.5).then_inc(rs_ready.sem, 1)
                if e in qk_sums:
                    k = qk_sums.index(e)
                    act.wait_ge(rs_ready.sem, rs_ready.by(layer, e + 1))
                    if k >= 2:
                        act.wait_ge(qk_ready.sem, qk_ready.by(layer, k - 1))
                    activate(newton[:, k % 2, :], rs[:, e % 2, :], ACT.Square).then_inc(rs_squared.sem, 1)

            def exps(layer, t):
                h, part = STEPS[t]
                act.wait_ge(neg_max_ready.sem, neg_max_ready.by(layer, t + 1))
                if t >= 1:
                    act.wait_ge(a_ready.sem, a_ready.by(layer, t))
                for b, (i, c0) in enumerate(PARTS[part]):
                    n = (i + 1) * P
                    for j in range(2):
                        last = activate(probs[:, j, c0:c0 + n], sc_ps[:, j, c0:c0 + n], ACT.Exp,
                                        bias=neg_mx[:, t % 2, 2 * b + j:2 * b + j + 1], scale=DH ** -0.5,
                                        accum_out=p_sum[:, t % 2, 2 * b + j:2 * b + j + 1])
                last.then_inc(probs_ready.sem, 1)

            def copy_aT(layer, t):
                n = sum(i + 1 for i, _ in PARTS[STEPS[t][1]]) * P
                act.wait_ge(transposed.sem, transposed.by(layer, t + 1))
                if t >= 2:
                    act.wait_ge(pv_done.sem, pv_done.by(layer, t - 1))
                activate(aT[:, t % 2, 0:n], t_ps[:, 0:n], ACT.Copy).then_inc(aT_ready.sem, 1)

            def gate_logs(layer, p):
                tmp = gate_tmp[:, p, :]
                act.wait_ge(z_done.sem, z_done.by(layer, p + 1))
                activate(tmp, bank_of(("z", p))[:, :], ACT.Abs).then_inc(z_abs.sem, 1)
                act.wait_ge(z_abs.sem, z_abs.by(layer, p + 1))
                activate(tmp, tmp, ACT.Exp, scale=-1.0).then_inc(z_exp.sem, 1)
                act.wait_ge(z_exp.sem, z_exp.by(layer, p + 1))
                activate(tmp, tmp, ACT.Ln, bias=one).then_inc(z_log.sem, 1)

            def key_decays(layer, p):
                act.wait_ge(suffix_done.sem, suffix_done.by(layer, p + 1))
                act.wait_ge(la_ready.sem, la_ready.by(layer, p + 1))
                activate(kd_tmp[:, p, :], bank_of(("suf", p))[:, :], ACT.Exp, scale=1.0 / TAU).then_inc(kd_ready.sem, 1)

            def chunk_decays(layer, p):
                act.wait_ge(decay_done.sem, decay_done.by(layer, p + 1))
                activate(decay[:, p, :], bank_of(("dec", p))[:, 0:NC], ACT.Exp, scale=1.0 / TAU)\
                    .then_inc(decay_ready.sem, 1)

            def silu_r(layer, h):
                act.wait_ge(rg_ready.sem, rg_ready.by(layer, h + 1))
                r = act_lo_f32[:, head_slot(f"g{h}"), :]
                activate(r, r, ACT.Silu).then_inc(silu_done.sem, 1)

            def head_hi(layer, name, count, value):
                k = OUT_ORDER.index(name)
                act.wait_ge(count.sem, count.by(layer, value))
                slot = head_slot(name)
                activate(act_hi[:, slot, :], act_lo_f32[:, slot, :], ACT.Copy).then_inc(o_hi_ready.sem, 1)

            with act.Fori(0, L) as layer:
                for u, (kind, n) in enumerate(MIXER_UNITS):
                    split_hi(layer, 0, u + AHEAD)
                    if u - 1 in STEP_AT:
                        copy_aT(layer, STEP_AT[u - 1])
                    if u == 0:
                        rsqrt_mean(layer, 0, rbc[:, :], o_ps[:, :], D)
                        rsqrt_mean(layer, 1, rtok[:, :], sc_ps[:, 0, 0:TT], D)
                    if kind in ("q", "k"):
                        square_qk(layer, f"{kind}{n}")
                    for name, at_unit in HEADS_LEAVE:
                        if at_unit == u:
                            copy_and_square_head(layer, name)
                    for e, (name, at_unit) in enumerate(SUMS):
                        if at_unit == u:
                            rsqrt_sum(layer, e)
                    if u in STEP_AT:
                        exps(layer, STEP_AT[u])
                    if u == 10:
                        gate_logs(layer, 0)
                        gate_logs(layer, 1)
                    if u == 13:
                        key_decays(layer, 0)
                        key_decays(layer, 1)
                    if u == 14:
                        chunk_decays(layer, 0)
                        chunk_decays(layer, 1)
                    if u == 12:
                        head_hi(layer, "d0", o_normed, 1)
                    if u == 15:
                        head_hi(layer, "d1", o_normed, 2)
                    if u == 18:
                        head_hi(layer, "d2", o_normed, 3)
                    if u == 21:
                        silu_r(layer, 0)
                        silu_r(layer, 1)
                        exp_and_ln()
                    if u == 22:
                        head_hi(layer, "g0", gated, 1)
                        head_hi(layer, "g1", gated, 2)
                head_hi(layer, "d3", o_normed, 8)
                silu_r(layer, 2)
                silu_r(layer, 3)
                head_hi(layer, "g2", gated, 3)
                head_hi(layer, "g3", gated, 4)
                with act.Fori(0, KT // SLOTS) as i:
                    for s in range(SLOTS):
                        split_hi(layer, i * SLOTS + U_OUT, s + AHEAD)
                        act.wait_ge(x_ready.sem, x_ready.by(layer, i * SLOTS + s + 1))
                        normed_tile(layer, i * SLOTS + KT + s, i * SLOTS + s, layer * KT + i * SLOTS + C_N2 + s)

                def conv_col(tap, i, s):
                    return layer * (4 * 2 * FT) + i * 2 + (C_CONV + tap * 2 * FT + s // 2 + (s % 2) * FT)

                def up_stage(i, s, first):
                    n = i * SLOTS + s
                    split_hi(layer, i * SLOTS + U_UP, s + AHEAD)
                    act.wait_ge(u_ready.sem, u_ready.by(layer, n + 1))
                    if not first:
                        act.wait_ge(act_lo_ready.sem, act_lo_ready.by(layer, i * 2 - 2 + s // 2 + 1))
                    activate(c_buf[:, s, :], u_buf[:, s, 2:T + 2], ACT.Identity,
                             scale=params[:, bass.ds(conv_col(2, i, s), 1)],
                             bias=params[:, bass.ds(conv_col(3, i, s), 1)]).then_inc(tap2_done.sem, 1)
                    if s % 2 == 1:
                        act.wait_ge(conv_done.sem, conv_done.by(layer, n))
                        activate(c_buf[:, s - 1, :], c_buf[:, s - 1, :], ACT.Silu).then_inc(gate_ready.sem, 1)
                    elif s > 0 or not first:
                        hi_of_product(i * 2 + (s // 2 - 1), (s - 1) % SLOTS)

                def hi_of_product(j, s):
                    act.wait_ge(product_ready.sem, product_ready.by(layer, j + 1))
                    activate(act_hi[:, j, :], c_buf[:, s, :], ACT.Copy).then_inc(act_hi_ready.sem, 1)

                exp_and_ln()
                rsqrt_mean(layer, 2, rbc[:, :], o_ps[:, :], D)
                nc.scalar.preload_act_table(ACT.Silu)
                for s in range(SLOTS):
                    up_stage(0, s, True)
                with act.Fori(1, 2 * FT // SLOTS) as i:
                    for s in range(SLOTS):
                        up_stage(i, s, False)
                hi_of_product(FT - 1, SLOTS - 1)
                exp_and_ln()
                with act.Fori(0, KT // SLOTS) as i:
                    for s in range(SLOTS):
                        for j in range(3):
                            split_hi(layer, i * 3 * SLOTS + U_DOWN, 3 * s + j + AHEAD)
                        act.wait_ge(x_ready.sem, x_ready.by(layer, i * SLOTS + KT + s + 1))
                        act.dma_start(out[i * SLOTS + s], x[:, i * SLOTS + s, :]).then_inc(stored, 16)
                        normed_tile(layer, i * SLOTS + 2 * KT + s, i * SLOTS + s,
                                    layer * KT + i * SLOTS + C_N1 + KT + s)
            act.wait_ge(stored, 16 * L * KT)

        @block.vector
        def _(dve):
            def tt(out_, a, b, op):
                return nc.vector.tensor_tensor(out_, a, b, op)

            def stt(out_, a, scalar, b, op0, op1):
                return nc.vector.scalar_tensor_tensor(out=out_, in0=a, scalar=scalar, in1=b, op0=op0, op1=op1)

            def normed_lo(layer, k, m, g_col):
                dve.wait_ge(h_hi_ready.sem, h_hi_ready.by(layer, k + 1))
                stt(h_lo[:, m, :], x[:, m, :], params[:, bass.ds(g_col, 1)], h_hi[:, m, :].bitcast(F32),
                    ALU.mult, ALU.subtract).then_inc(h_lo_ready.sem, 1)

            nc.vector.memset(acc[:, :], 0.0).then_inc(acc_zeroed.sem, 1)
            nc.vector.memset(ones_buf[:, :], 1.0).then_inc(ones_ready, 1)
            dve.wait_ge(params_landed, 16)
            tt(lam_prod[:, :], params[:, C_LAMQ:C_LAMQ + 2 * L], params[:, C_LAMK:C_LAMK + 2 * L], ALU.mult)\
                .then_inc(lam_prod_ready, 1)
            for m in range(KT):
                normed_lo(0, m, m, C_N1 + m)
                dve.wait_ge(sqx_ready.sem, m + 1)
                dve.wait_ge(acc_zeroed.sem, 1)
                dve.wait_ge(acc_added.sem, m)
                tt(acc[:, :], acc[:, :], sqx[:, :], ALU.add).then_inc(acc_added.sem, 1)
            dve.wait_ge(consts_landed, 48)
            tt(sub_g[:, :], params[:, C_SUB:C_SUB + L], consts[:, C_ONEMINUS:C_ONEMINUS + L], ALU.mult)\
                .then_inc(lam_steps, 1)
            dve.wait_ge(lam_exp_ready, 1)
            tt(lam_diff[:, :], lam_exp[:, 0:L], lam_exp[:, L:2 * L], ALU.subtract).then_inc(lam_steps, 1)
            dve.wait_ge(lam_steps, 2)
            stt(neg_lam[:, :], lam_diff[:, :], -1.0, consts[:, C_LAMINIT:C_LAMINIT + L], ALU.mult, ALU.subtract)\
                .then_inc(lam_steps, 1)
            dve.wait_ge(lam_steps, 3)

            def prepare_layer(layer):
                low = low_raw[:, layer, :]
                nc.vector.tensor_copy(low_hi, low).then_inc(layer_ready.sem, 1)
                nc.vector.tensor_copy(gk_up_now, gk_up[:, layer, :]).then_inc(layer_ready.sem, 1)
                nc.vector.memset(low_t, 1.0).then_inc(layer_ready.sem, 1)
                dve.wait_ge(layer_ready.sem, layer_ready.by(layer, 3))
                tt(low_lo, low, low_hi.bitcast(F32), ALU.subtract).then_inc(layer_ready.sem, 1)

            def leave_psum(layer, u):
                kind, n = MIXER_UNITS[u]
                dve.wait_ge(unit_done.sem, unit_done.by(layer, u + 1))
                if kind in ("dv", "gv", "gk"):
                    if n % 2 == 1:
                        g = n // 2
                        dve.wait_ge(r_ready.sem, r_ready.by(layer, 2))
                        for t in range(TT):
                            src = bank_of((kind, 2 * g + t // 2))[:, t % 2 * 256:t % 2 * 256 + 256]
                            dst, count = {"dv": (vd[:, t, g * 256:g * 256 + 256], v_ready),
                                          "gv": (vg[:, t, g * 256:g * 256 + 256], gv_ready),
                                          "gk": (kg[:, t // 2, t % 2 * 256:t % 2 * 256 + 256], gk_ready)}[kind]
                            nc.vector.tensor_scalar(dst, src, rtok[:, t:t + 1], None, ALU.mult).then_inc(count.sem, 1)
                    return
                dst, count = {"q": (qk[:, 2 * n, :], qk_raw), "k": (qk[:, 2 * n + 1, :], qk_raw),
                              "gq": (gq[:, n % 2, :], gq_ready),
                              "r": (act_lo_f32[:, head_slot(f"g{n}"), :], rg_ready)}[kind]
                dve.wait_ge(r_ready.sem, r_ready.by(layer, 1))
                tt(dst, bank_of((kind, n))[:, :], rbc[:, :], ALU.mult).then_inc(count.sem, 1)

            def maxima(layer, t):
                h, part = STEPS[t]
                blocks = PARTS[part]
                dve.wait_ge(scores_done.sem, scores_done.by(layer, t + 1))
                for i, c0 in blocks:
                    hidden = c0 + i * P + CHUNK
                    last = nc.vector.memset(sc_ps[0:CHUNK, :, hidden:hidden + CHUNK], NEG)
                last.then_inc(masked.sem, 1)
                dve.wait_ge(masked.sem, masked.by(layer, t + 1))
                for b, (i, c0) in enumerate(blocks):
                    last = nc.vector.tensor_reduce(mx[:, t % 2, 2 * b:2 * b + 2], sc_ps[:, :, c0:c0 + (i + 1) * P],
                                                   AX_X, ALU.max)
                last.then_inc(max_done.sem, 1)
                dve.wait_ge(max_done.sem, max_done.by(layer, t + 1))
                n = 2 * len(blocks)
                nc.vector.tensor_scalar(neg_mx[:, t % 2, 0:n], mx[:, t % 2, 0:n], -DH ** -0.5, None, ALU.mult)\
                    .then_inc(neg_max_ready.sem, 1)

            def combine(layer, t):
                h, part = STEPS[t]
                blocks = PARTS[part]
                n = len(blocks)
                dve.wait_ge(probs_ready.sem, probs_ready.by(layer, t + 1))
                nc.vector.reciprocal(p_rec[:, t % 2, 0:2 * n], p_sum[:, t % 2, 0:2 * n]).then_inc(rec_ready.sem, 1)
                dve.wait_ge(rec_ready.sem, rec_ready.by(layer, t + 1))
                odd = p_rec[:, t % 2, 0:2 * n].rearrange("p (b j) -> p b j", j=2)[:, :, 1]
                nc.vector.tensor_scalar(p_lam[:, t % 2, 0:n], odd, neg_lam[:, bass.ds(layer, 1)], None, ALU.mult)\
                    .then_inc(lam_scaled.sem, 1)
                if t >= 2:
                    dve.wait_ge(transposed.sem, transposed.by(layer, t - 1))
                for b, (i, c0) in enumerate(blocks):
                    cols = slice(c0, c0 + (i + 1) * P)
                    last = nc.vector.tensor_scalar(a_buf[:, t % 2, cols], probs[:, 0, cols],
                                                   p_rec[:, t % 2, 2 * b:2 * b + 1], None, ALU.mult)
                last.then_inc(a_half.sem, 1)
                dve.wait_ge(lam_scaled.sem, lam_scaled.by(layer, t + 1))
                dve.wait_ge(a_half.sem, a_half.by(layer, t + 1))
                for b, (i, c0) in enumerate(blocks):
                    cols = slice(c0, c0 + (i + 1) * P)
                    last = stt(a_buf[:, t % 2, cols], probs[:, 1, cols], p_lam[:, t % 2, b:b + 1],
                               a_buf[:, t % 2, cols], ALU.mult, ALU.add)
                last.then_inc(a_ready.sem, 1)

            def apply_norm(layer, e):
                name = SUMS[e][0]
                h = int(name[1])
                if name[0] in "qk":
                    t, g, count = (qk[:, 2 * h + (name[0] == "k"), :],
                                   params[:, bass.ds(layer + (C_QG if name[0] == "q" else C_KG), 1)], qk_ready)
                elif name[0] == "d":
                    t, g, count = act_lo_f32[:, head_slot(name), :], sub_g[:, bass.ds(layer, 1)], o_normed
                else:
                    t, g, count = act_hi_f32[:, head_slot(name), :], params[:, bass.ds(layer + C_GG, 1)], o_normed
                dve.wait_ge(rs_ready.sem, rs_ready.by(layer, e + 1))
                if name[0] in "dg":
                    stt(t, t, g, rs[:, e % 2, :], ALU.mult, ALU.mult).then_inc(count.sem, 1)
                    return
                k = qk_sums.index(e) + 1
                stt(t, t, g, rs[:, e % 2, :], ALU.mult, ALU.mult).then_inc(qk_scaled.sem, 1)
                dve.wait_ge(rs_squared.sem, rs_squared.by(layer, k))
                step = newton[:, (k - 1) % 2, :]
                stt(step, bank_of(("sum", e))[:, :], DH * EPS, step, ALU.add, ALU.mult)\
                    .then_inc(newton_product.sem, 1)
                dve.wait_ge(newton_product.sem, newton_product.by(layer, k))
                nc.vector.tensor_scalar(step, step, -0.5 / DH, 1.5, ALU.mult, ALU.add)\
                    .then_inc(newton_factor.sem, 1)
                dve.wait_ge(qk_scaled.sem, qk_scaled.by(layer, k))
                dve.wait_ge(newton_factor.sem, newton_factor.by(layer, k))
                tt(t, t, step, ALU.mult).then_inc(count.sem, 1)

            def log_gates(layer, p):
                dve.wait_ge(z_log.sem, z_log.by(layer, p + 1))
                stt(la[:, p, :], bank_of(("z", p))[:, :], 0.0, gate_tmp[:, p, :], ALU.min, ALU.subtract)\
                    .then_inc(la_ready.sem, 1)

            def decay_keys(layer, p):
                dve.wait_ge(kd_ready.sem, kd_ready.by(layer, p + 1))
                dve.wait_ge(gk_ready.sem, gk_ready.by(layer, TT))
                tt(kg[:, p, :], kg[:, p, :], kd_tmp[:, p, :], ALU.mult).then_inc(k_decayed.sem, 1)

            def next_state(layer, c):
                dve.wait_ge(kv_done.sem, kv_done.by(layer, c + 1))
                kv = bank_of(("kv", c))[:, :].rearrange("p (a n) -> p a n", a=2)
                if c == 0:
                    for r in range(2):
                        last = nc.vector.tensor_copy(state[r * DK:(r + 1) * DK, 0, :, :],
                                                     kv[r * DK:(r + 1) * DK, :, r * DV:(r + 1) * DV])
                else:
                    dve.wait_ge(decay_ready.sem, decay_ready.by(layer, 2))
                    dve.wait_ge(state_ready.sem, state_ready.by(layer, c))
                    for r in range(2):
                        rows = slice(r * DK, (r + 1) * DK)
                        for a in range(2):
                            last = stt(state[rows, c, a, :], state[rows, c - 1, a, :], decay[rows, a, c:c + 1],
                                       kv[rows, a, r * DV:(r + 1) * DV], ALU.mult, ALU.add)
                last.then_inc(state_ready.sem, 1)

            def gate_head(layer, h):
                slot = head_slot(f"g{h}")
                dve.wait_ge(silu_done.sem, silu_done.by(layer, h + 1))
                dve.wait_ge(o_normed.sem, o_normed.by(layer, RS_USED[SUM_OF[f"g{h}"]][1]))
                tt(act_lo_f32[:, slot, :], act_lo_f32[:, slot, :], act_hi_f32[:, slot, :], ALU.mult)\
                    .then_inc(gated.sem, 1)

            def head_lo(layer, name):
                slot = head_slot(name)
                dve.wait_ge(o_hi_ready.sem, o_hi_ready.by(layer, OUT_ORDER.index(name) + 1))
                tt(act_lo[:, slot, :], act_lo_f32[:, slot, :], act_hi[:, slot, :].bitcast(F32), ALU.subtract)\
                    .then_inc(o_lo_ready.sem, 1)

            with dve.Fori(0, L) as layer:
                prepare_layer(layer)
                for u in range(U_OUT):
                    leave_psum(layer, u)
                    if u == 9:
                        dve.wait_ge(low_done.sem, low_done.by(layer, 1))
                        dve.wait_ge(layer_ready.sem, layer_ready.by(layer, 4))
                        tt(low_t[0:RANK, :], bank_of(("low", 0))[0:RANK, :], rbc[0:RANK, :], ALU.mult)\
                            .then_inc(low_ready.sem, 1)
                    if u in STEP_AT:
                        maxima(layer, STEP_AT[u])
                    for e, (name, at_unit) in enumerate(SUMS):
                        if at_unit == u:
                            apply_norm(layer, e)
                    if u == 10:
                        log_gates(layer, 0)
                        log_gates(layer, 1)
                    if u in STEP_AT:
                        combine(layer, STEP_AT[u])
                    if u == 13:
                        decay_keys(layer, 0)
                        decay_keys(layer, 1)
                    if 16 <= u < 20:
                        next_state(layer, 2 * (u - 16))
                        next_state(layer, 2 * (u - 16) + 1)
                    if u in (12, 15, 18):
                        head_lo(layer, f"d{(u - 12) // 3}")
                    if u == 22:
                        gate_head(layer, 0)
                        gate_head(layer, 1)
                        head_lo(layer, "g0")
                        head_lo(layer, "g1")
                head_lo(layer, "d3")
                gate_head(layer, 2)
                gate_head(layer, 3)
                head_lo(layer, "g2")
                head_lo(layer, "g3")

                dve.wait_ge(stored, layer * (16 * KT))
                dve.wait_ge(tokens_summed.sem, tokens_summed.by(layer, 2))
                nc.vector.memset(acc[:, :], 0.0).then_inc(acc_zeroed.sem, 1)
                with dve.Fori(0, KT // SLOTS) as i:
                    for s in range(SLOTS):
                        m = i * SLOTS + s
                        dve.wait_ge(unit_done.sem, unit_done.by(layer, i * SLOTS + (U_OUT + s + 1)))
                        tt(x[:, m, :], x[:, m, :], bank[s][:, :], ALU.add).then_inc(x_ready.sem, 1)
                        dve.wait_ge(x_ready.sem, x_ready.by(layer, m + 1))
                        normed_lo(layer, m + KT, m, layer * KT + i * SLOTS + (C_N2 + s))

                nc.vector.memset(u_buf[:, :, 0:2], 0.0).then_inc(pads_zeroed.sem, 1)
                dve.wait_ge(pads_zeroed.sem, pads_zeroed.by(layer, 1))
                dve.wait_ge(r_ready.sem, r_ready.by(layer, 3))

                def conv_col(tap, i, s):
                    return layer * (4 * 2 * FT) + i * 2 + (C_CONV + tap * 2 * FT + s // 2 + (s % 2) * FT)

                def convolve(i, s):
                    n = i * SLOTS + s
                    dve.wait_ge(tap2_done.sem, tap2_done.by(layer, n + 1))
                    stt(c_buf[:, s, :], u_buf[:, s, 1:T + 1], params[:, bass.ds(conv_col(1, i, s), 1)], c_buf[:, s, :],
                        ALU.mult, ALU.add).then_inc(tap1_done.sem, 1)
                    dve.wait_ge(tap1_done.sem, tap1_done.by(layer, n + 1))
                    stt(c_buf[:, s, :], u_buf[:, s, 0:T], params[:, bass.ds(conv_col(0, i, s), 1)], c_buf[:, s, :],
                        ALU.mult, ALU.add).then_inc(conv_done.sem, 1)

                def product(j, n, s):
                    dve.wait_ge(gate_ready.sem, gate_ready.by(layer, j + 1))
                    dve.wait_ge(conv_done.sem, conv_done.by(layer, n + 1))
                    tt(c_buf[:, s, :], c_buf[:, s, :], c_buf[:, s - 1, :], ALU.mult).then_inc(product_ready.sem, 1)

                def lo_of_product(j, s):
                    dve.wait_ge(act_hi_ready.sem, act_hi_ready.by(layer, j + 1))
                    tt(act_lo[:, j, :], c_buf[:, s, :], act_hi[:, j, :].bitcast(F32), ALU.subtract)\
                        .then_inc(act_lo_ready.sem, 1)

                def up_stage(i, s, first):
                    n = i * SLOTS + s
                    dve.wait_ge(unit_done.sem, unit_done.by(layer, n + (U_UP + 1)))
                    tt(u_buf[:, s, 2:T + 2], bank[s][:, :], rbc[:, :], ALU.mult).then_inc(u_ready.sem, 1)
                    if s == 3:
                        lo_of_product(i * 2, 1)
                    if s == 1 and not first:
                        lo_of_product(i * 2 - 1, 3)
                    if s > 0:
                        convolve(i, s - 1)
                    elif not first:
                        convolve(i - 1, 3)
                    if s == 2:
                        product(i * 2, n - 1, 1)
                    if s == 0 and not first:
                        product(i * 2 - 1, n - 1, 3)

                for s in range(SLOTS):
                    up_stage(0, s, True)
                with dve.Fori(1, 2 * FT // SLOTS) as i:
                    for s in range(SLOTS):
                        up_stage(i, s, False)
                convolve(2 * FT // SLOTS - 1, 3)
                product(FT - 1, 2 * FT - 1, 3)
                lo_of_product(FT - 1, 3)

                dve.wait_ge(tokens_summed.sem, tokens_summed.by(layer, 3))
                nc.vector.memset(acc[:, :], 0.0).then_inc(acc_zeroed.sem, 1)
                with dve.Fori(0, KT // SLOTS) as i:
                    for s in range(SLOTS):
                        m = i * SLOTS + s
                        dve.wait_ge(unit_done.sem, unit_done.by(layer, i * (3 * SLOTS) + (U_DOWN + 3 * (s + 1))))
                        tt(x[:, m, :], x[:, m, :], bank[s][:, :], ALU.add).then_inc(x_ready.sem, 1)
                        dve.wait_ge(x_ready.sem, x_ready.by(layer, m + KT + 1))
                        normed_lo(layer, m + 2 * KT, m, layer * KT + i * SLOTS + (C_N1 + KT + s))

        @block.tensor
        def _(pe):
            def mm(out_, lhsT, rhs, start, stop, **kw):
                return nc.tensor.matmul(out_, lhsT, rhs, start=start, stop=stop, **kw)

            def three(out_, hi, lo, rhs_hi, rhs_lo, start, stop, **kw):
                mm(out_, hi, rhs_hi, start, False, **kw)
                mm(out_, lo, rhs_hi, False, False, **kw)
                return mm(out_, hi, rhs_lo, False, stop, **kw)

            def weights(s, k):
                return w_hi[:, s, k * P:(k + 1) * P], w_lo[:, s, k * P:(k + 1) * P]

            def middle(layer, u):
                if u - 2 in STEP_AT:
                    values(layer, STEP_AT[u - 2])

            def rows_tile(layer, u):
                kind, n = MIXER_UNITS[u]
                s = u % SLOTS
                pe.wait_ge(lo_ready.sem, lo_ready.by(layer, u + 1))
                b = take_bank(layer, (kind, n))
                for k in range(KT):
                    if k == KT // 2:
                        middle(layer, u)
                    last = three(b[:, :], *weights(s, k), h_hi[:, k, :], h_lo[:, k, :], k == 0, k == KT - 1)
                last.then_inc(unit_done.sem, 1)

            def token_tiles(layer, u):
                kind, n = MIXER_UNITS[u]
                s = u % SLOTS
                pe.wait_ge(lo_ready.sem, lo_ready.by(layer, u + 1))
                if n % 2 == 0:
                    take_two(layer, (kind, n))
                g = n // 2
                for kk in range(KT // 2):
                    k = n % 2 * (KT // 2) + kk
                    if kk == KT // 4:
                        middle(layer, u)
                    if u < 2:
                        pe.wait_ge(h_lo_ready.sem, h_lo_ready.by(layer, k + 1))
                    whi, wlo = (w[:, s, kk * 256:(kk + 1) * 256] for w in (w_hi, w_lo))
                    for t in range(TT):
                        o = bank_of((kind, 2 * g + t // 2))[:, t % 2 * 256:t % 2 * 256 + 256]
                        tok = slice(t * P, (t + 1) * P)
                        first, end = k == 0 and t % 2 == 0, k == KT - 1
                        mm(o, h_hi[:, k, tok], whi, first, False, skip_group_check=True)
                        mm(o, h_hi[:, k, tok], wlo, False, False, skip_group_check=True)
                        last = mm(o, h_lo[:, k, tok], whi, False, end, skip_group_check=True)
                last.then_inc(unit_done.sem, 1)

            def sum_tokens(layer, added):
                pe.wait_ge(acc_added.sem, acc_added.by(layer, added))
                mm(o_ps[:, :], ones, acc[:, :], True, True).then_inc(tokens_summed.sem, 1)

            def scores(layer, t):
                h, part = STEPS[t]
                pe.wait_ge(qk_ready.sem, qk_ready.by(layer, 2 * h + 2))
                pe.wait_ge(probs_ready.sem, probs_ready.by(layer, t))
                if t == 0:
                    pe.wait_ge(ln_tokens.sem, ln_tokens.by(layer, 2))
                for i, c0 in PARTS[part]:
                    for j in range(2):
                        rows = slice(j * DH, (j + 1) * DH)
                        last = mm(sc_ps[:, j, c0:c0 + (i + 1) * P], qk[rows, 2 * h, i * P:(i + 1) * P],
                                  qk[rows, 2 * h + 1, 0:(i + 1) * P], True, True)
                last.then_inc(scores_done.sem, 1)

            def transposes(layer, t):
                pe.wait_ge(a_ready.sem, a_ready.by(layer, t + 1))
                pe.wait_ge(aT_ready.sem, aT_ready.by(layer, t))
                if t == 0:
                    pe.wait_ge(lam_exp_ready, 1)
                n = 0
                for i, c0 in PARTS[STEPS[t][1]]:
                    for j in range(i + 1):
                        last = nc.tensor.transpose(t_ps[:, n * P:(n + 1) * P],
                                                   a_buf[:, t % 2, c0 + j * P:c0 + (j + 1) * P], ident)
                        n += 1
                last.then_inc(transposed.sem, 1)

            def values(layer, t):
                h, part = STEPS[t]
                pe.wait_ge(aT_ready.sem, aT_ready.by(layer, t + 1))
                pe.wait_ge(v_ready.sem, v_ready.by(layer, 2 * TT))
                if part == 0:
                    if h == 0:
                        pe.wait_ge(ln_tokens.sem, ln_tokens.by(layer, 1))
                    else:
                        pe.wait_ge(squared.sem, squared.by(layer, SUM_OF[f"d{h - 1}"] + 1))
                n = 0
                for i, _ in PARTS[part]:
                    for j in range(i + 1):
                        last = mm(o_ps[:, i * P:(i + 1) * P], vd[:, j, h * DV:(h + 1) * DV],
                                  aT[:, t % 2, n * P:(n + 1) * P], j == 0, j == i)
                        n += 1
                last.then_inc(pv_done.sem, 1)

            def small(layer, kind, n):
                if kind == "ss":
                    pe.wait_ge(ln_tokens.sem, ln_tokens.by(layer, 0))
                    sum_tokens(layer, KT)
                elif kind == "rtok":
                    pe.wait_ge(probs_ready.sem, probs_ready.by(layer, 0))
                    for t in range(TT):
                        last = mm(sc_ps[:, 0, t:t + 1], acc[:, t * P:(t + 1) * P], ones[:, 0:1], True, True)
                    last.then_inc(tokens_summed.sem, 1)
                elif kind == "T":
                    transposes(layer, n)
                elif kind == "scores":
                    scores(layer, n)
                elif kind == "sum":
                    b = take_bank(layer, ("sum", n))
                    if n == 0:
                        pe.wait_ge(consts_landed, 48)
                    pe.wait_ge(squared.sem, squared.by(layer, n + 1))
                    m = same_map if SUMS[n][0][0] in "qk" else ones
                    mm(b[:, :], m, sq[:, n % 2, :], True, True).then_inc(summed.sem, 1)
                elif kind == "low":
                    b = take_bank(layer, ("low", 0))
                    pe.wait_ge(layer_ready.sem, layer_ready.by(layer, 4))
                    for k in range(KT):
                        cols = slice(k * RANK, (k + 1) * RANK)
                        last = three(b[0:RANK, :], low_hi[:, cols], low_lo[:, cols], h_hi[:, k, :], h_lo[:, k, :],
                                     k == 0, k == KT - 1)
                    last.then_inc(low_done.sem, 1)
                elif kind == "z":
                    b = take_bank(layer, ("z", n))
                    pe.wait_ge(low_ready.sem, low_ready.by(layer, 1))
                    for t in range(2):
                        tok = (2 * n + t) * P
                        last = mm(b[:, t * 256:(t + 1) * 256], low_t[:, tok:tok + P], gk_up_now, True, True)
                    last.then_inc(z_done.sem, 1)
                elif kind == "suf":
                    b = take_bank(layer, ("suf", n))
                    pe.wait_ge(la_ready.sem, la_ready.by(layer, n + 1))
                    mm(b[:, :], later, la[:, n, :], True, True).then_inc(suffix_done.sem, 1)
                elif kind == "dec":
                    b = take_bank(layer, ("dec", n))
                    pe.wait_ge(la_ready.sem, la_ready.by(layer, 2))
                    for t in range(TT):
                        c0 = t % 2 * 256 + n * P
                        last = mm(b[:, 2 * t:2 * t + 2], la[:, t // 2, c0:c0 + P], halves, True, True)
                    last.then_inc(decay_done.sem, 1)
                elif kind == "kv":
                    b = take_bank(layer, ("kv", n))
                    pe.wait_ge(k_decayed.sem, k_decayed.by(layer, 2))
                    pe.wait_ge(gv_ready.sem, gv_ready.by(layer, 2 * TT))
                    t, rows = n // 2, slice(n % 2 * CHUNK, (n % 2 + 1) * CHUNK)
                    for a in range(2):
                        c0 = t % 2 * 256 + a * P
                        last = mm(b[:, a * 256:(a + 1) * 256], kg[rows, t // 2, c0:c0 + P],
                                  vg[rows, t, a * 256:(a + 1) * 256], True, True)
                    last.then_inc(kv_done.sem, 1)
                elif kind == "go":
                    b = take_bank(layer, ("go", n))
                    pe.wait_ge(state_ready.sem, state_ready.by(layer, NC))
                    pe.wait_ge(gq_ready.sem, gq_ready.by(layer, n // 2 + 1))
                    rows = slice(n % 2 * DK, (n % 2 + 1) * DK)
                    for c in range(NC):
                        cols = slice(c * CHUNK, (c + 1) * CHUNK)
                        last = mm(b[:, cols], state[rows, c, n // 2, :], gq[rows, n // 2, cols], True, True)
                    last.then_inc(go_done.sem, 1)

            pe.wait_ge(lam_prod_ready, 1)
            pe.wait_ge(ones_ready, 1)
            mm(t_ps[:, 0:2 * L], ones, lam_prod[:, :], True, True).then_inc(lam_summed, 1)

            with pe.Fori(0, L) as layer:
                for u in range(U_OUT):
                    if MIXER_UNITS[u][0] in ("dv", "gk", "gv"):
                        token_tiles(layer, u)
                    else:
                        rows_tile(layer, u)
                    for kind, n in small_items(u):
                        small(layer, kind, n)

                with pe.Fori(0, KT // SLOTS) as i:
                    for s in range(SLOTS):
                        pe.wait_ge(lo_ready.sem, lo_ready.by(layer, i * SLOTS + (U_OUT + s + 1)))
                        mixers_use, k = FREED[RING[s - SLOTS]]
                        pe.wait_ge(mixers_use.sem, mixers_use.by(layer, k))
                        pe.wait_ge(h_lo_ready.sem, h_lo_ready.by(layer, i * SLOTS + (KT - SLOTS + s + 1)))
                        for j, name in enumerate(OUT_ORDER):
                            k = head_slot(name)
                            if s == 0:
                                pe.wait_ge(o_lo_ready.sem, o_lo_ready.by(layer, j + 1))
                            last = three(bank[s][:, :], *weights(s, k), act_hi[:, k, :], act_lo[:, k, :],
                                         j == 0, j == KT - 1)
                        last.then_inc(unit_done.sem, 1)

                def up_unit(i, s, first):
                    pe.wait_ge(lo_ready.sem, lo_ready.by(layer, i * SLOTS + (U_UP + s + 1)))
                    free = 2 * KT - SLOTS + s + 1
                    if first and s > 0:
                        pe.wait_ge(h_lo_ready.sem, h_lo_ready.by(layer, free))
                    if not first:
                        pe.wait_ge(u_ready.sem, u_ready.by(layer, i * SLOTS + (s - SLOTS + 1)))
                    for k in range(KT):
                        if first and s == 0:
                            pe.wait_ge(h_lo_ready.sem, h_lo_ready.by(layer, max(KT + k + 1, free)))
                        last = three(bank[s][:, :], *weights(s, k), h_hi[:, k, :], h_lo[:, k, :], k == 0, k == KT - 1)
                    last.then_inc(unit_done.sem, 1)

                for s in range(SLOTS):
                    up_unit(0, s, True)
                    if s == 0:
                        pe.wait_ge(squared.sem, squared.by(layer, SUM_OF["d3"] + 1))
                        sum_tokens(layer, 2 * KT)
                with pe.Fori(1, 2 * FT // SLOTS) as i:
                    for s in range(SLOTS):
                        up_unit(i, s, False)

                with pe.Fori(0, KT // SLOTS) as i:
                    for s in range(SLOTS):
                        pe.wait_ge(u_ready.sem, u_ready.by(layer, 2 * FT - SLOTS + s + 1))
                        pe.wait_ge(x_ready.sem, x_ready.by(layer, i * SLOTS + (KT - SLOTS + s + 1)))
                        j = 0
                        for c, blocks in enumerate(DOWN_BLOCKS):
                            slot = (3 * s + c) % SLOTS
                            pe.wait_ge(lo_ready.sem, lo_ready.by(layer, i * (3 * SLOTS) + (U_DOWN + 3 * s + c + 1)))
                            for k in range(blocks):
                                if s == 0:
                                    pe.wait_ge(act_lo_ready.sem, act_lo_ready.by(layer, j + 1))
                                last = three(bank[s][:, :], *weights(slot, k), act_hi[:, j, :], act_lo[:, j, :],
                                             j == 0, j == FT - 1)
                                j += 1
                            last.then_inc(unit_done.sem, 1)


def units_of_weights(w_in, w_out, w_up, w_down):
    starts = np.concatenate([[0], np.cumsum(IN_SPLITS)])
    first = dict(zip(("gq", "gk", "gv", "r", "low", "q", "k", "dv"), starts))

    def columns(w, c0):
        return w[:, c0:c0 + P].reshape(-1, P, P).transpose(1, 0, 2).reshape(P, -1)

    units = []
    for layer in range(L):
        for kind, n in MIXER_UNITS:
            c0 = first[kind]
            if kind in ("dv", "gk", "gv"):
                rows = w_in[layer, n % 2 * (D // 2):(n % 2 + 1) * (D // 2), c0 + n // 2 * 256:c0 + n // 2 * 256 + 256]
                units.append(rows.reshape(KT // 2, P, 256).transpose(1, 0, 2).reshape(P, -1))
            else:
                units.append(columns(w_in[layer], c0 + n * P))
        units += [columns(w_out[layer], m * P) for m in range(KT)]
        for j in range(FT):
            units += [columns(w_up[layer], j * P), columns(w_up[layer], FF + j * P)]
        for m in range(KT):
            whole = columns(w_down[layer], m * P)
            k = 0
            for blocks in DOWN_BLOCKS:
                part = whole[:, k * P:(k + blocks) * P]
                units.append(np.pad(part, ((0, 0), (0, 1024 - blocks * P))))
                k += blocks
    units += [np.zeros((P, 1024), np.float32)] * AHEAD
    low = w_in[:, :, first["low"]:first["low"] + RANK].reshape(L, KT, P, RANK).transpose(2, 0, 1, 3).reshape(P, L, -1)
    return np.stack(units), low


def columns_of_params(inputs):
    def tiles(a):
        return a.reshape(-1, P).T

    cols = [tiles(inputs["norm1_g"]), np.zeros((P, KT), np.float32), tiles(inputs["norm2_g"])]
    for layer in range(L):
        cols += [tiles(inputs["ffn_conv_w"][layer]), tiles(inputs["ffn_conv_b"][layer])]
    cols += [tiles(inputs["gla_norm_g"]), tiles(inputs["diff_sub_g"])]
    cols += [np.tile(inputs[k].T, (2, 1)) for k in ("diff_q_norm_g", "diff_k_norm_g")]
    cols += [np.pad(inputs[k].T, ((0, P - DH), (0, 0))) for k in ("diff_lam_q1", "diff_lam_q2", "diff_lam_k1", "diff_lam_k2")]
    return np.concatenate(cols, axis=1)


def constants():
    row, col = np.arange(P)[:, None], np.arange(P)[None, :]
    same = row // CHUNK == col // CHUNK
    init = [0.8 - 0.6 * float(np.exp(-0.3 * layer)) for layer in range(L)]
    cols = [row == col, same, same & (row > col), row // CHUNK == np.arange(2)[None, :],
            np.full((P, 1), EPS), np.tile([init], (P, 1)), np.tile([[1.0 - v for v in init]], (P, 1))]
    return np.concatenate([np.asarray(c, np.float32) for c in cols], axis=1)


def kernel(**inputs):
    import concourse.bacc as bacc
    from concourse.bass_utils import run_bass_kernel_spmd

    inputs = {k: np.asarray(v) for k, v in inputs.items()}
    units, low = units_of_weights(inputs["w_in"], inputs["w_out"], inputs["ffn_w_up"], inputs["ffn_w_down"])
    gk_up = np.concatenate([inputs["gla_w_gk_up"], inputs["gla_b_gk"][:, None, :]], axis=1).transpose(1, 0, 2)
    arrays = {
        "in_x": inputs["x"][0].T.reshape(KT, P, T), "in_units": units, "in_low": low, "in_gk_up": gk_up,
        "in_params": columns_of_params(inputs), "in_consts": constants(),
    }
    arrays = {k: np.ascontiguousarray(v) for k, v in arrays.items()}
    nc = bacc.Bacc("TRN2", target_bir_lowering=False, num_devices=1)
    args = [nc.dram_tensor(k, v.shape, mybir.dt.from_np(v.dtype), kind="ExternalInput").ap() for k, v in arrays.items()]
    args.append(nc.dram_tensor("out_x", (KT, P, T), F32, kind="ExternalOutput").ap())
    trunk(nc, *args)
    r = run_bass_kernel_spmd(nc, [arrays], core_ids=[0])
    return r.results[0]["out_x"].reshape(D, T).T.reshape(1, T, D)
```

```python
from contextlib import ExitStack

import concourse.bass as bass
import numpy as np
from concourse import mybir

F32 = mybir.dt.float32
F32R = mybir.dt.float32r
ALU = mybir.AluOpType
ACT = mybir.ActivationFunctionType
AX_X = mybir.AxisListType.X

P = 128
D = 1024
T = 512
L = 2
CHUNK = 64
EPS = 1e-6
KT = D // P
TT = T // P
NC = T // CHUNK
H = 4
DK = 64
DV = 128
DH = 64
RANK = 16
LOW_ROWS = 2 * RANK + 1
TAU = 16.0
FF = 2816
FT = FF // P
IN_SPLITS = (H * DK, H * DK, H * DV, H * DV, RANK, 2 * H * DH, 2 * H * DH, H * DV)
AHEAD = 3
FIRST_PARTS = KT // 2
RAW = 2
SLOTS = 4
DOWN_BLOCKS = (8, 8, 6)
NEG = -1.0e30

X_LOADS = [(0, 1), (1, 2), (2, 4), (4, 6), (6, 8)]
CONSTS_LANDED = 3 * 16

MIXER_UNITS = [("dv", 0), ("dv", 1), ("dv", 2), ("dv", 3), ("q", 0), ("k", 0), ("q", 1), ("k", 1),
               ("q", 2), ("k", 2), ("gk", 0), ("gk", 1), ("gv", 0), ("gv", 1), ("gv", 2), ("gv", 3),
               ("q", 3), ("k", 3), ("gq", 0), ("gq", 1), ("r", 0), ("r", 1), ("r", 2), ("r", 3)]
U_OUT = len(MIXER_UNITS)
U_UP = U_OUT + KT
U_DOWN = U_UP + 2 * FT
UNITS = U_DOWN + 3 * KT
assert UNITS % SLOTS == 0 and U_OUT % SLOTS == 0 and U_UP % SLOTS == 0 and U_DOWN % SLOTS == 0
UNIT_OF = {x: u for u, x in enumerate(MIXER_UNITS)}

PARTS = [[(0, 0), (1, 128)], [(2, 0)], [(3, 0)]]
STEPS = [(h, part) for h in range(H) for part in range(len(PARTS))]



def mid(u):
    return 2 * u


def end(u):
    return 2 * u + 1


PLACES = 2 * U_OUT
MID_TILE = 5
SCORES = [mid(u) for u in range(7, 16)] + [mid(19), end(19), end(20)]
TRANSPOSES = [place + 3 for place in SCORES]
VALUES = [place + 1 for place in TRANSPOSES]
GLA_OUT = [end(19), mid(20), end(20), mid(21)]
SUMS = [("q0", mid(5)), ("k0", mid(6)), ("q1", mid(7)), ("k1", mid(8)), ("q2", mid(9)), ("k2", mid(10)),
        ("d0", end(12)), ("d1", mid(15)), ("q3", mid(17)), ("d2", mid(18)), ("k3", mid(18)), ("g0", end(20)),
        ("g1", mid(21)), ("g2", end(21)), ("g3", mid(22)), ("d3", mid(23))]
SUM_OF = {name: e for e, (name, _) in enumerate(SUMS)}
OTHERS = {end(1): [("ss", 0), ("rtok", 0)], mid(11): [("low", 0)], mid(14): [("z", 0), ("z", 1)],
          mid(15): [("suf", 0)], end(15): [("suf", 1)], mid(16): [("dec", 0)],
          end(16): [("kv", 0), ("kv", 1)], mid(17): [("kv", 2), ("kv", 3)], end(17): [("kv", 4), ("kv", 5)],
          mid(18): [("kv", 6)], end(18): [("kv", 7)]}
OUT_ORDER = ["d0", "d1", "d2", "g0", "g1", "d3", "g2", "g3"]
HEAD_SPLIT = {mid(13): "d0", end(15): "d1", end(18): "d2", end(23): "d3"}
OUT_TILE = {**{f"g{h}": h for h in range(H)}, **{f"d{h}": H + h for h in range(H)}}


def small_items(place):
    items = [("T", t) for t, at in enumerate(TRANSPOSES) if at == place]
    items += [("values", t) for t, at in enumerate(VALUES) if at == place]
    items += [("sum", e) for e, (_, at) in enumerate(SUMS) if at == place]
    items += OTHERS.get(place, [])
    items += [("go", h) for h, at in enumerate(GLA_OUT) if at == place]
    return items + [("scores", t) for t, at in enumerate(SCORES) if at == place]


def squares_at(place):
    u = place // 2
    names = ["%s%d" % MIXER_UNITS[u]] if place == end(u) and MIXER_UNITS[u][0] in ("q", "k") else []
    for kind, n in small_items(place):
        if kind == "values" and STEPS[n][1] == len(PARTS) - 1:
            names.append(f"d{STEPS[n][0]}")
        elif kind == "go":
            names.append(f"g{n}")
    return [SUM_OF[name] for name in names]


BANK_LAG = {"dv": 0.7, "gk": 0.7, "gv": 0.7, "q": 0.4, "k": 0.4, "gq": 0.4, "r": 0.4, "sum": 1.6, "low": 0.4, "z": 1.2,
            "suf": 0.6, "dec": 0.6, "kv": 1.0, "go": 0.6}


def share_banks():
    uses = []
    for u, (kind, n) in enumerate(MIXER_UNITS):
        if kind in ("dv", "gk", "gv"):
            if n % 2 == 0:
                uses += [((kind, n), end(u - 1), end(u + 1)), ((kind, n + 1), end(u - 1), end(u + 1))]
        else:
            uses.append(((kind, n), end(u - 1), end(u)))
        uses += [(x, at, at) for at in (mid(u), end(u)) for x in small_items(at)
                 if x[0] in ("low", "z", "sum", "suf", "dec", "kv", "go")]
    free_at = [-4.0, -3.0, -2.0, -1.0]
    banks, before, last_in = {}, {}, [None] * 4
    for use, first, last in uses:
        b = min(range(4), key=lambda b: free_at[b])
        assert free_at[b] <= first + BANK_LAG[use[0]] + 1, (use, free_at)
        banks[use], before[use] = b, last_in[b]
        last_in[b], free_at[b] = use, last + BANK_LAG[use[0]]
    return banks, before, last_in, sorted(range(4), key=lambda b: free_at[b])


BANK_OF, USE_BEFORE, LAST_IN, ROUND = share_banks()
DOWN_ROUND = [1, 0, 3, 2]
assert DOWN_ROUND[0] != ROUND[3]

C_N1 = 0
C_N2 = C_N1 + (L + 1) * KT
C_CONV = C_N2 + L * KT
C_GG = C_CONV + L * 4 * 2 * FT
C_SUB = C_GG + L
C_QG = C_SUB + L
C_KG = C_QG + L
C_LAMQ = C_KG + L
C_LAMK = C_LAMQ + 2 * L
N_PARAMS = C_LAMK + 2 * L
C_IDENT, C_BLOCKS, C_LATER = 0, P, 2 * P
C_HALVES = 3 * P
C_EPS = C_HALVES + 2
C_LAMINIT = C_EPS + 1
C_ONEMINUS = C_LAMINIT + L
N_CONSTS = C_ONEMINUS + L


def trunk(nc, x_in, units, low_in, gk_up_in, params_in, consts_in, out):
    with ExitStack() as ctx:
        base = nc.sbuf_base
        base += -base % 32
        at = [base]

        def place(name, shape, dt=F32, where=None):
            size = 4 * int(np.prod(shape[1:]))
            t = nc.alloc_sbuf_tensor_at(name, shape, dt, offset=at[0] if where is None else where)
            if where is None:
                at[0] += size + -size % 32
            return t

        x = place("x", [P, KT, T])
        h_hi = place("h_hi", [P, KT, T], F32R)
        h_lo = place("h_lo", [P, KT, T], F32R)
        raw = place("raw", [P, RAW, 1024])
        w_hi = place("w_hi", [P, SLOTS, 1024], F32R)
        w_lo = place("w_lo", [P, SLOTS, 1024], F32R)
        at_act_hi = at[0]
        act_hi = place("act_hi", [P, FT, T], F32R)
        at_act_lo = at[0]
        act_lo = place("act_lo", [P, FT, T], F32R)
        act_hi_f32 = place("act_hi_f32", [P, KT, T], F32, at_act_hi)
        act_lo_f32 = place("act_lo_f32", [P, KT, T], F32, at_act_lo)
        a0 = at_act_hi + 4 * KT * T
        vd = place("vd", [P, TT, T], F32, a0)
        vg = place("vg", [P, TT, T], F32, a0 + 8192)
        kg = place("kg", [P, 2, T], F32, a0 + 16384)
        gq = place("gq", [P, 2, T], F32, a0 + 20480)
        la = place("la", [P, 2, T], F32, a0 + 24576)
        b0 = at_act_lo + 4 * KT * T
        qk = place("qk", [P, 2 * H, T], F32, b0)
        qk_lo = place("qk_lo", [P, 2 * H, T], F32R, b0)
        state = place("state", [P, NC, 2, DV], F32, b0 + 16384)
        probs = place("probs", [P, 2, T], F32, b0 + 24576)
        at_c = at[0]
        u_buf = place("u_buf", [P, SLOTS, T + 2])
        c_buf = place("c_buf", [P, SLOTS, T])
        a_buf = place("a_buf", [P, 2, T], F32, at_c)
        aT = place("aT", [P, 2, T], F32, at_c + 4096)
        sq = place("sq", [P, 2, T], F32, at_c + 8192)
        sq_lo = place("sq_lo", [P, 2, T], F32R, at_c + 8192)
        rs = place("rs", [P, 2, T], F32, at_c + 12288)
        ones_r = place("ones_r", [P, P], F32R)
        rbc = place("rbc", [P, T])
        acc = place("acc", [P, T])
        at_sqx = at[0]
        sqx = place("sqx", [P, 2, T])[:, 0, :]
        sq_hi = place("sq_hi", [P, 2, T], F32R, at_sqx)
        low_raw = place("low_raw", [P, L, KT * RANK])
        params = place("params", [P, N_PARAMS])
        at_consts = at[0]
        consts = place("consts", [P, N_CONSTS])
        same_map_r = place("same_map_r", [P, P], F32R, at_consts + 4 * C_BLOCKS)
        gk_up = place("gk_up", [LOW_ROWS, L, H * DK])
        rtok = place("rtok", [P, TT])
        neg_lam = place("neg_lam", [P, L])
        sub_g = place("sub_g", [P, L])
        qk_g = place("qk_g", [P, 2 * L])
        lam_prod = place("lam_prod", [P, 2 * L])
        lam_exp = place("lam_exp", [P, 2 * L])
        lam_diff = place("lam_diff", [P, L])
        mx = place("mx", [P, 2, 4])
        neg_mx = place("neg_mx", [P, 2, 4])
        p_sum = place("p_sum", [P, 2, 4])
        p_rec = place("p_rec", [P, 2, 4])
        p_lam = place("p_lam", [P, 2, 2])
        decay = place("decay", [P, 2, NC])
        assert at[0] <= nc.sbuf_usable_end, (at[0], nc.sbuf_usable_end)
        low_pair = act_lo[:, 6, 0:2 * KT * RANK].rearrange("p (k j n) -> p k j n", k=KT, j=2)
        gk_up_now = act_hi_f32[0:LOW_ROWS, 2, 0:H * DK]
        low_t = act_hi_f32[0:LOW_ROWS, 3, :]
        newton = act_lo_f32[:, 0:2, :]
        gate_tmp = act_hi_f32[:, 6:8, :]
        kd_tmp = act_hi_f32[:, 6:8, :]

        ident = consts[:, C_IDENT:C_IDENT + P]
        same_map = consts[:, C_BLOCKS:C_BLOCKS + P]
        later = consts[:, C_LATER:C_LATER + P]
        ones = ones_r[:, :].bitcast(F32)
        halves = consts[:, C_HALVES:C_HALVES + 2]
        eps = consts[:, C_EPS:C_EPS + 1]
        one = ones[:, 0:1]

        bank = [ctx.enter_context(nc.psum_tensor(f"bank{b}", [P, T], F32)) for b in range(4)]
        sc_ps = ctx.enter_context(nc.psum_tensor("sc_ps", [P, 2, T], F32))
        t_ps = ctx.enter_context(nc.psum_tensor("t_ps", [P, T], F32))
        o_ps = ctx.enter_context(nc.psum_tensor("o_ps", [P, T], F32))

        class Count:

            def __init__(self, name, each, start=0):
                self.sem, self.each, self.start = ctx.enter_context(nc.semaphore(name)), each, start

            def by(self, layer, k):
                return layer * self.each + (self.start + k)

        def sem(name):
            return ctx.enter_context(nc.semaphore(name))

        x_landed = [sem(f"x_landed{m}") for m in range(len(X_LOADS))]
        params_landed = sem("params_landed")
        raw_landed = [sem(f"raw_landed{s}") for s in range(RAW)]
        lam_prod_ready, lam_summed, lam_exp_ready = sem("lam_prod_ready"), sem("lam_summed"), sem("lam_exp_ready")
        lam_steps, ones_ready, map_ready = sem("lam_steps"), sem("ones_ready"), sem("map_ready")
        act_moved = sem("act_moved")
        first_hi_half, first_lo_quarters = sem("first_hi_half"), sem("first_lo_quarters")
        hi_ready = Count("hi_ready", UNITS)
        lo_ready = Count("lo_ready", UNITS)
        unit_done = Count("unit_done", UNITS)
        x_ready = Count("x_ready", 2 * KT, start=SLOTS)
        h_hi_ready = Count("h_hi_ready", 2 * KT)
        h_lo_ready = Count("h_lo_ready", 2 * KT)
        sqx_ready = Count("sqx_ready", 2 * KT)
        acc_zeroed = Count("acc_zeroed", 2)
        acc_added = Count("acc_added", 2 * KT)
        tokens_summed = Count("tokens_summed", 3)
        ln_tokens = Count("ln_tokens", 3)
        r_ready = Count("r_ready", 3)
        layer_ready = Count("layer_ready", 4)
        v_ready = Count("v_ready", 2 * TT)
        gk_ready = Count("gk_ready", TT)
        gv_ready = Count("gv_ready", 2 * TT)
        qk_raw = Count("qk_raw", 2 * H)
        qk_ready = Count("qk_ready", 2 * H)
        gq_ready = Count("gq_ready", 2)
        rg_ready = Count("rg_ready", H)
        squared = Count("squared", len(SUMS))
        squares_split = Count("squares_split", len(SUMS))
        summed = Count("summed", len(SUMS))
        ln_done = Count("ln_done", len(SUMS))
        rs_ready = Count("rs_ready", len(SUMS))
        rs_squared = Count("rs_squared", 2 * H)
        newton_product = Count("newton_product", 2 * H)
        qk_scaled = Count("qk_scaled", 2 * H)
        qk_hi_ready = Count("qk_hi_ready", 2 * H)
        qk_lo_ready = Count("qk_lo_ready", 2 * H)
        o_copied = Count("o_copied", 2 * H)
        o_normed = Count("o_normed", 2 * H)
        gated = Count("gated", H)
        silu_done = Count("silu_done", H)
        o_hi_ready = Count("o_hi_ready", 2 * H)
        o_lo_ready = Count("o_lo_ready", 2 * H)
        n_steps = len(STEPS)
        scores_done = Count("scores_done", n_steps)
        masked = Count("masked", n_steps)
        max_done = Count("max_done", n_steps)
        neg_max_ready = Count("neg_max_ready", n_steps)
        probs_ready = Count("probs_ready", n_steps)
        rec_ready = Count("rec_ready", n_steps)
        lam_scaled = Count("lam_scaled", n_steps)
        a_half = Count("a_half", n_steps)
        a_ready = Count("a_ready", n_steps)
        transposed = Count("transposed", n_steps)
        aT_ready = Count("aT_ready", n_steps)
        pv_done = Count("pv_done", n_steps)
        low_done = Count("low_done", 1)
        low_ready = Count("low_ready", 1)
        z_done = Count("z_done", 2)
        z_abs = Count("z_abs", 2)
        z_exp = Count("z_exp", 2)
        z_log = Count("z_log", 2)
        la_ready = Count("la_ready", 2)
        suffix_done = Count("suffix_done", 2)
        kd_ready = Count("kd_ready", 2)
        k_decayed = Count("k_decayed", 2)
        decay_done = Count("decay_done", 1)
        decay_ready = Count("decay_ready", 1)
        kv_done = Count("kv_done", NC)
        state_ready = Count("state_ready", NC)
        go_done = Count("go_done", H)
        pads_zeroed = Count("pads_zeroed", 1)
        u_ready = Count("u_ready", 2 * FT)
        tap2_done = Count("tap2_done", 2 * FT)
        tap1_done = Count("tap1_done", 2 * FT)
        conv_done = Count("conv_done", 2 * FT)
        gate_ready = Count("gate_ready", FT)
        product_ready = Count("product_ready", FT)
        act_hi_ready = Count("act_hi_ready", FT)
        act_lo_ready = Count("act_lo_ready", FT)

        qk_sums = [e for e, (name, _) in enumerate(SUMS) if name[0] in "qk"]
        o_sums = [e for e, (name, _) in enumerate(SUMS) if name[0] in "dg"]

        def qk_hi(h, j):
            return act_hi[:, j, :] if h % 2 == 0 else act_lo[:, 2 + j, :]

        def given_back(use):
            kind, n = use
            return {
                "dv": lambda: (v_ready, TT * (n // 2) + 2 * (n % 2) + 2), "gk": lambda: (gk_ready, 2 * n + 2),
                "gv": lambda: (gv_ready, TT * (n // 2) + 2 * (n % 2) + 2),
                "q": lambda: (qk_raw, 2 * n + 1), "k": lambda: (qk_raw, 2 * n + 2),
                "gq": lambda: (gq_ready, n + 1), "r": lambda: (rg_ready, n + 1),
                "low": lambda: (low_ready, 1),
                "z": lambda: (la_ready, n + 1), "suf": lambda: (kd_ready, n + 1),
                "dec": lambda: (decay_ready, n + 1), "kv": lambda: (state_ready, n + 1),
                "sum": lambda: (newton_product, qk_sums.index(n) + 1) if n in qk_sums else (ln_done, n + 1),
                "go": lambda: (o_copied, RS_USED[SUM_OF[f"g{n}"]][1]),
            }[kind]()

        RS_USED = {**{e: (qk_scaled, k + 1) for k, e in enumerate(qk_sums)},
                   **{e: (o_normed, k + 1) for k, e in enumerate(o_sums)}}

        def freed(use):
            before = USE_BEFORE[use]
            return given_back(before) if before else (x_ready, DOWN_ROUND.index(BANK_OF[use]) + 1 - SLOTS)

        def take_bank(layer, use):
            last_use, k = freed(use)
            nc.tensor.wait_ge(last_use.sem, last_use.by(layer, k))
            return bank[BANK_OF[use]]

        def take_two(layer, use):
            (a, k), (b, j) = freed(use), freed((use[0], use[1] + 1))
            if a is b:
                k = max(k, j)
            else:
                nc.tensor.wait_ge(b.sem, b.by(layer, j))
            nc.tensor.wait_ge(a.sem, a.by(layer, k))

        def bank_of(use):
            return bank[BANK_OF[use]]

        def head_slot(name):
            return OUT_TILE[name]

        block = ctx.enter_context(nc.Block())

        @block.sync
        def _(sp):
            def load(n, s):
                sp.dma_start(raw[:, s, :], units[n]).then_inc(raw_landed[s], 16)

            sp.dma_start(params[:, :], params_in).then_inc(params_landed, 16)
            load(0, 0)
            for n, (a, b) in enumerate(X_LOADS):
                if n > 0:
                    sp.dma_start(x[:, a:b, :], x_in[:, a:b, :]).then_inc(x_landed[n], 16)
                if n == 2:
                    load(1, 1)
            sp.wait_ge(first_lo_quarters, FIRST_PARTS - 1)
            with sp.Fori(1, L * UNITS // RAW + 1) as i:
                for s in range(RAW):
                    sp.wait_ge(lo_ready.sem, (i - 1) * RAW + s + 1)
                    load(i * RAW + s, s)
            last = L * UNITS + RAW
            for n in range(last, L * UNITS + AHEAD):
                sp.wait_ge(lo_ready.sem, n - RAW + 1)
                load(n, n % RAW)
            for s in range(RAW):
                sp.wait_ge(raw_landed[s], 16 * len(range(s, L * UNITS + AHEAD, RAW)))

        @block.gpsimd
        def _(pool):
            def split_lo(layer, u0, s):
                slot = s % SLOTS
                pool.wait_ge(hi_ready.sem, hi_ready.by(layer, u0 + s + 1))
                nc.gpsimd.tensor_tensor(w_lo[:, slot, :], raw[:, slot % RAW, :], w_hi[:, slot, :].bitcast(F32),
                                        ALU.subtract).then_inc(lo_ready.sem, 1)

            def add_square(layer, k, zeroed):
                pool.wait_ge(sqx_ready.sem, sqx_ready.by(layer, k + 1))
                pool.wait_ge(acc_zeroed.sem, acc_zeroed.by(layer, zeroed))
                pool.wait_ge(acc_added.sem, acc_added.by(layer, k))
                nc.gpsimd.tensor_tensor(acc[:, :], acc[:, :], sqx, ALU.add).then_inc(acc_added.sem, 1)

            def split_square(layer, e):
                pool.wait_ge(squared.sem, squared.by(layer, e + 1))
                nc.gpsimd.tensor_tensor(sq_lo[:, e % 2, :], sq[:, e % 2, :], sq_hi[:, e % 2, :].bitcast(F32),
                                        ALU.subtract).then_inc(squares_split.sem, 1)

            for quarter in range(FIRST_PARTS):
                cols = slice(quarter * 1024 // FIRST_PARTS, (quarter + 1) * 1024 // FIRST_PARTS)
                if quarter < FIRST_PARTS // 2:
                    pool.wait_ge(first_hi_half, 1)
                else:
                    pool.wait_ge(hi_ready.sem, 1)
                done = first_lo_quarters if quarter > 0 else lo_ready.sem
                nc.gpsimd.tensor_tensor(w_lo[:, 0, cols], raw[:, 0, cols], w_hi[:, 0, cols].bitcast(F32),
                                        ALU.subtract).then_inc(done, 1)
            for n in range(1, AHEAD):
                split_lo(0, 0, n)
            with pool.Fori(0, L) as layer:
                for place in range(PLACES):
                    for e in squares_at(place):
                        split_square(layer, e)
                    if place % 2 == 1:
                        split_lo(layer, 0, place // 2 + AHEAD)
                with pool.Fori(0, KT // SLOTS) as i:
                    for s in range(SLOTS):
                        split_lo(layer, i * SLOTS + U_OUT, s + AHEAD)
                        add_square(layer, i * SLOTS + KT + s, 2)
                with pool.Fori(0, 2 * FT // SLOTS) as i:
                    for s in range(SLOTS):
                        split_lo(layer, i * SLOTS + U_UP, s + AHEAD)
                with pool.Fori(0, KT // SLOTS) as i:
                    for s in range(SLOTS):
                        for j in range(3):
                            split_lo(layer, i * 3 * SLOTS + U_DOWN, 3 * s + j + AHEAD)
                        add_square(layer, i * SLOTS + 2 * KT + s, 3)

        @block.scalar
        def _(act):
            def activate(*args, **kw):
                return nc.scalar.activation(*args, **kw)

            def split_hi(layer, u0, s):
                slot = s % SLOTS
                act.wait_ge(raw_landed[slot % RAW],
                            layer * (UNITS // RAW * 16) + u0 * (16 // RAW) + (s // RAW + 1) * 16)
                if not (isinstance(u0, int) and u0 + s < SLOTS):
                    act.wait_ge(unit_done.sem, unit_done.by(layer, u0 + (s - SLOTS + 1)))
                activate(w_hi[:, slot, :], raw[:, slot % RAW, :], ACT.Copy).then_inc(hi_ready.sem, 1)

            def normed_tile(layer, k, m, g_col):
                if not isinstance(k, int):
                    act.wait_ge(acc_added.sem, acc_added.by(layer, k))
                activate(h_hi[:, m, :], x[:, m, :], ACT.Copy, scale=params[:, bass.ds(g_col, 1)])\
                    .then_inc(h_hi_ready.sem, 1)
                if isinstance(k, int) and k > 0:
                    act.wait_ge(acc_added.sem, k)
                activate(sqx, x[:, m, :], ACT.Square).then_inc(sqx_ready.sem, 1)

            def rsqrt_mean(layer, which, dst, src, width):
                act.wait_ge(tokens_summed.sem, tokens_summed.by(layer, which + 1))
                activate(dst, src, ACT.Ln, scale=1.0 / width, bias=eps).then_inc(ln_tokens.sem, 1)
                act.wait_ge(ln_tokens.sem, ln_tokens.by(layer, which + 1))
                activate(dst, dst, ACT.Exp, scale=-0.5).then_inc(r_ready.sem, 1)

            def exp_and_ln():
                nc.scalar.preload_act_table_set("natural_log_exp_and_others")

            a, b = X_LOADS[0]
            act.dma_start(x[:, a:b, :], x_in[:, a:b, :]).then_inc(x_landed[0], 16)
            exp_and_ln()
            act.wait_ge(params_landed, 16)
            for m in range(KT):
                for n, (a, b) in enumerate(X_LOADS):
                    if m == a:
                        act.wait_ge(x_landed[n], 16)
                normed_tile(0, m, m, C_N1 + m)
                if m == 0:
                    act.wait_ge(raw_landed[0], 16)
                    activate(w_hi[:, 0, 0:512], raw[:, 0, 0:512], ACT.Copy).then_inc(first_hi_half, 1)
                    activate(w_hi[:, 0, 512:1024], raw[:, 0, 512:1024], ACT.Copy).then_inc(hi_ready.sem, 1)
                if m == 3:
                    split_hi(0, 0, 1)
                if m == 1:
                    for dst, src in ((consts[:, :], consts_in), (low_raw[:, :, :], low_in), (gk_up[:, :, :], gk_up_in)):
                        act.dma_start(dst, src).then_inc(act_moved, 16)
            split_hi(0, 0, 2)
            act.wait_ge(act_moved, CONSTS_LANDED)
            act.wait_ge(lam_summed, 1)
            activate(lam_exp[:, :], t_ps[:, 0:2 * L], ACT.Exp).then_inc(lam_exp_ready, 1)

            def square_qk(layer, name):
                e = SUM_OF[name]
                j = 2 * int(name[1]) + (name[0] == "k")
                act.wait_ge(qk_raw.sem, qk_raw.by(layer, j + 1))
                if e >= 2:
                    act.wait_ge(summed.sem, summed.by(layer, e - 1))
                activate(sq_hi[:, e % 2, :], qk[:, j, :], ACT.Square)
                activate(sq[:, e % 2, :], qk[:, j, :], ACT.Square).then_inc(squared.sem, 1)

            def copy_and_square_head(layer, name):
                e, h = SUM_OF[name], int(name[1])
                if name[0] == "d":
                    act.wait_ge(pv_done.sem, pv_done.by(layer, len(PARTS) * (h + 1)))
                    src, dst, scale = o_ps, act_lo_f32[:, head_slot(name), :], 1.0
                else:
                    act.wait_ge(go_done.sem, go_done.by(layer, h + 1))
                    src, dst, scale = bank_of(("go", h)), act_hi_f32[:, head_slot(name), :], DK ** -0.5
                if e >= 2:
                    act.wait_ge(summed.sem, summed.by(layer, e - 1))
                activate(sq_hi[:, e % 2, :], src[:, :], ACT.Square, scale=scale)
                activate(sq[:, e % 2, :], src[:, :], ACT.Square, scale=scale).then_inc(squared.sem, 1)
                activate(dst, src[:, :], ACT.Copy, scale=scale).then_inc(o_copied.sem, 1)

            def rsqrt_sum(layer, e):
                name = SUMS[e][0]
                width = DH if name[0] in "qk" else DV
                act.wait_ge(summed.sem, summed.by(layer, e + 1))
                if e >= 2:
                    last_use, k = RS_USED[e - 2]
                    act.wait_ge(last_use.sem, last_use.by(layer, k))
                activate(rs[:, e % 2, :], bank_of(("sum", e))[:, :], ACT.Ln, scale=1.0 / width, bias=eps)\
                    .then_inc(ln_done.sem, 1)
                act.wait_ge(ln_done.sem, ln_done.by(layer, e + 1))
                activate(rs[:, e % 2, :], rs[:, e % 2, :], ACT.Exp, scale=-0.5).then_inc(rs_ready.sem, 1)
                if e in qk_sums:
                    k = qk_sums.index(e)
                    act.wait_ge(rs_ready.sem, rs_ready.by(layer, e + 1))
                    if k >= 2:
                        act.wait_ge(qk_ready.sem, qk_ready.by(layer, k - 1))
                    activate(newton[:, k % 2, :], rs[:, e % 2, :], ACT.Square).then_inc(rs_squared.sem, 1)

            def qk_to_hi(layer, k):
                act.wait_ge(qk_ready.sem, qk_ready.by(layer, k + 1))
                activate(qk_hi(k // 2, k % 2), qk[:, k, :], ACT.Copy).then_inc(qk_hi_ready.sem, 1)

            def exps(layer, t):
                h, part = STEPS[t]
                act.wait_ge(neg_max_ready.sem, neg_max_ready.by(layer, t + 1))
                if t >= 1:
                    act.wait_ge(a_ready.sem, a_ready.by(layer, t))
                for b, (i, c0) in enumerate(PARTS[part]):
                    n = (i + 1) * P
                    for j in range(2):
                        last = activate(probs[:, j, c0:c0 + n], sc_ps[:, j, c0:c0 + n], ACT.Exp,
                                        bias=neg_mx[:, t % 2, 2 * b + j:2 * b + j + 1], scale=DH ** -0.5,
                                        accum_out=p_sum[:, t % 2, 2 * b + j:2 * b + j + 1])
                last.then_inc(probs_ready.sem, 1)

            def copy_aT(layer, t):
                n = sum(i + 1 for i, _ in PARTS[STEPS[t][1]]) * P
                act.wait_ge(transposed.sem, transposed.by(layer, t + 1))
                if t >= 2:
                    act.wait_ge(pv_done.sem, pv_done.by(layer, t - 1))
                activate(aT[:, t % 2, 0:n], t_ps[:, 0:n], ACT.Copy).then_inc(aT_ready.sem, 1)

            def gate_logs(layer, p):
                tmp = gate_tmp[:, p, :]
                act.wait_ge(z_done.sem, z_done.by(layer, p + 1))
                activate(tmp, bank_of(("z", p))[:, :], ACT.Abs).then_inc(z_abs.sem, 1)
                act.wait_ge(z_abs.sem, z_abs.by(layer, p + 1))
                activate(tmp, tmp, ACT.Exp, scale=-1.0).then_inc(z_exp.sem, 1)
                act.wait_ge(z_exp.sem, z_exp.by(layer, p + 1))
                activate(tmp, tmp, ACT.Ln, bias=one).then_inc(z_log.sem, 1)

            def key_decays(layer, p):
                act.wait_ge(suffix_done.sem, suffix_done.by(layer, p + 1))
                act.wait_ge(la_ready.sem, la_ready.by(layer, p + 1))
                activate(kd_tmp[:, p, :], bank_of(("suf", p))[:, :], ACT.Exp, scale=1.0 / TAU).then_inc(kd_ready.sem, 1)

            def chunk_decays(layer):
                act.wait_ge(decay_done.sem, decay_done.by(layer, 1))
                activate(decay[:, :, :], bank_of(("dec", 0))[:, 0:2 * NC].rearrange("p (a c) -> p a c", a=2),
                         ACT.Exp, scale=1.0 / TAU)\
                    .then_inc(decay_ready.sem, 1)

            def silu_r(layer, h):
                act.wait_ge(rg_ready.sem, rg_ready.by(layer, h + 1))
                r = act_lo_f32[:, head_slot(f"g{h}"), :]
                activate(r, r, ACT.Silu).then_inc(silu_done.sem, 1)

            def head_hi(layer, name, count, value):
                k = OUT_ORDER.index(name)
                act.wait_ge(count.sem, count.by(layer, value))
                slot = head_slot(name)
                activate(act_hi[:, slot, :], act_lo_f32[:, slot, :], ACT.Copy).then_inc(o_hi_ready.sem, 1)

            with act.Fori(0, L) as layer:
                for place in range(PLACES):
                    items = small_items(place)
                    u = place // 2
                    if place == end(u) and MIXER_UNITS[u][0] in ("q", "k"):
                        square_qk(layer, "%s%d" % MIXER_UNITS[u])
                    for kind, n in items:
                        if kind == "T":
                            copy_aT(layer, n)
                        elif kind == "values" and STEPS[n][1] == len(PARTS) - 1:
                            copy_and_square_head(layer, f"d{STEPS[n][0]}")
                        elif kind == "sum":
                            rsqrt_sum(layer, n)
                        elif kind == "go":
                            copy_and_square_head(layer, f"g{n}")
                        elif kind == "ss":
                            rsqrt_mean(layer, 0, rbc[:, :], o_ps[:, :], D)
                        elif kind == "rtok":
                            rsqrt_mean(layer, 1, rtok[:, :], sc_ps[:, 0, 0:TT], D)
                        elif kind == "z":
                            gate_logs(layer, n)
                        elif kind == "suf":
                            key_decays(layer, n)
                        elif kind == "dec":
                            chunk_decays(layer)
                        elif kind == "scores":
                            exps(layer, n)
                    for k, e in enumerate(qk_sums):
                        if SUMS[e][1] == place - 1:
                            qk_to_hi(layer, k)
                    if place == end(21):
                        nc.scalar.preload_act_table(ACT.Silu)
                        silu_r(layer, 0)
                        silu_r(layer, 1)
                        exp_and_ln()
                    if place == end(22):
                        head_hi(layer, "g0", gated, 1)
                        head_hi(layer, "g1", gated, 2)
                    if place == end(u) and u < U_OUT - 1:
                        split_hi(layer, 0, u + AHEAD)
                    if place == mid(23):
                        nc.scalar.preload_act_table(ACT.Silu)
                        silu_r(layer, 2)
                    if place in HEAD_SPLIT:
                        head_hi(layer, HEAD_SPLIT[place], o_normed, 1 + o_sums.index(SUM_OF[HEAD_SPLIT[place]]))
                silu_r(layer, 3)
                head_hi(layer, "g2", gated, 3)
                head_hi(layer, "g3", gated, 4)
                split_hi(layer, 0, U_OUT - 1 + AHEAD)
                with act.Fori(0, KT // SLOTS) as i:
                    for s in range(SLOTS):
                        split_hi(layer, i * SLOTS + U_OUT, s + AHEAD)
                        act.wait_ge(x_ready.sem, x_ready.by(layer, i * SLOTS + s + 1))
                        normed_tile(layer, i * SLOTS + KT + s, i * SLOTS + s, layer * KT + i * SLOTS + C_N2 + s)

                def conv_col(tap, i, s):
                    return layer * (4 * 2 * FT) + i * 2 + (C_CONV + tap * 2 * FT + s // 2 + (s % 2) * FT)

                def up_stage(i, s, first):
                    n = i * SLOTS + s
                    split_hi(layer, i * SLOTS + U_UP, s + AHEAD)
                    act.wait_ge(u_ready.sem, u_ready.by(layer, n + 1))
                    if not first:
                        act.wait_ge(act_lo_ready.sem, act_lo_ready.by(layer, i * 2 - 2 + s // 2 + 1))
                    activate(c_buf[:, s, :], u_buf[:, s, 2:T + 2], ACT.Identity,
                             scale=params[:, bass.ds(conv_col(2, i, s), 1)],
                             bias=params[:, bass.ds(conv_col(3, i, s), 1)]).then_inc(tap2_done.sem, 1)
                    if s % 2 == 1:
                        act.wait_ge(conv_done.sem, conv_done.by(layer, n))
                        activate(c_buf[:, s - 1, :], c_buf[:, s - 1, :], ACT.Silu).then_inc(gate_ready.sem, 1)
                    elif s > 0 or not first:
                        hi_of_product(i * 2 + (s // 2 - 1), (s - 1) % SLOTS)

                def hi_of_product(j, s):
                    act.wait_ge(product_ready.sem, product_ready.by(layer, j + 1))
                    activate(act_hi[:, j, :], c_buf[:, s, :], ACT.Copy).then_inc(act_hi_ready.sem, 1)

                exp_and_ln()
                rsqrt_mean(layer, 2, rbc[:, :], o_ps[:, :], D)
                nc.scalar.preload_act_table(ACT.Silu)
                for s in range(SLOTS):
                    up_stage(0, s, True)
                with act.Fori(1, 2 * FT // SLOTS) as i:
                    for s in range(SLOTS):
                        up_stage(i, s, False)
                hi_of_product(FT - 1, SLOTS - 1)
                exp_and_ln()
                with act.Fori(0, KT // SLOTS) as i:
                    for s in range(SLOTS):
                        for j in range(3):
                            split_hi(layer, i * 3 * SLOTS + U_DOWN, 3 * s + j + AHEAD)
                        act.wait_ge(x_ready.sem, x_ready.by(layer, i * SLOTS + KT + s + 1))
                        act.dma_start(out[i * SLOTS + s], x[:, i * SLOTS + s, :]).then_inc(act_moved, 16)
                        normed_tile(layer, i * SLOTS + 2 * KT + s, i * SLOTS + s,
                                    layer * KT + i * SLOTS + C_N1 + KT + s)
            act.wait_ge(act_moved, CONSTS_LANDED + 16 * L * KT)

        @block.vector
        def _(dve):
            def tt(out_, a, b, op):
                return nc.vector.tensor_tensor(out_, a, b, op)

            def stt(out_, a, scalar, b, op0, op1):
                return nc.vector.scalar_tensor_tensor(out=out_, in0=a, scalar=scalar, in1=b, op0=op0, op1=op1)

            def normed_lo(layer, k, m, g_col):
                dve.wait_ge(h_hi_ready.sem, h_hi_ready.by(layer, k + 1))
                stt(h_lo[:, m, :], x[:, m, :], params[:, bass.ds(g_col, 1)], h_hi[:, m, :].bitcast(F32),
                    ALU.mult, ALU.subtract).then_inc(h_lo_ready.sem, 1)

            nc.vector.memset(acc[:, :], 0.0).then_inc(acc_zeroed.sem, 1)
            nc.vector.memset(ones, 1.0).then_inc(ones_ready, 1)
            nc.vector.memset(rtok[:, :], 0.0).then_inc(x_ready.sem, x_ready.start)
            dve.wait_ge(params_landed, 16)
            tt(lam_prod[:, :], params[:, C_LAMQ:C_LAMQ + 2 * L], params[:, C_LAMK:C_LAMK + 2 * L], ALU.mult)\
                .then_inc(lam_prod_ready, 1)
            for m in range(KT):
                normed_lo(0, m, m, C_N1 + m)
                dve.wait_ge(sqx_ready.sem, m + 1)
                dve.wait_ge(acc_zeroed.sem, 1)
                if m > 0:
                    dve.wait_ge(acc_added.sem, m)
                tt(acc[:, :], acc[:, :], sqx, ALU.add).then_inc(acc_added.sem, 1)
            dve.wait_ge(act_moved, CONSTS_LANDED)
            nc.vector.tensor_copy(same_map_r[:, :], same_map).then_inc(map_ready, 1)
            tt(sub_g[:, :], params[:, C_SUB:C_SUB + L], consts[:, C_ONEMINUS:C_ONEMINUS + L], ALU.mult)\
                .then_inc(lam_steps, 1)
            nc.vector.tensor_scalar(qk_g[:, :], params[:, C_QG:C_QG + 2 * L], -0.5 / DH, None, ALU.mult)\
                .then_inc(lam_steps, 1)
            dve.wait_ge(lam_exp_ready, 1)
            tt(lam_diff[:, :], lam_exp[:, 0:L], lam_exp[:, L:2 * L], ALU.subtract).then_inc(lam_steps, 1)
            dve.wait_ge(lam_steps, 3)
            stt(neg_lam[:, :], lam_diff[:, :], -1.0, consts[:, C_LAMINIT:C_LAMINIT + L], ALU.mult, ALU.subtract)\
                .then_inc(lam_steps, 1)
            dve.wait_ge(lam_steps, 4)

            def prepare_layer(layer):
                low = low_raw[:, layer, :].rearrange("p (k n) -> p k n", k=KT)
                nc.vector.tensor_copy(low_pair[:, :, 0, :], low).then_inc(layer_ready.sem, 1)
                nc.vector.tensor_copy(gk_up_now, gk_up[:, layer, :]).then_inc(layer_ready.sem, 1)
                nc.vector.memset(low_t, 1.0).then_inc(layer_ready.sem, 1)
                dve.wait_ge(layer_ready.sem, layer_ready.by(layer, 3))
                tt(low_pair[:, :, 1, :], low, low_pair[:, :, 0, :].bitcast(F32), ALU.subtract)\
                    .then_inc(layer_ready.sem, 1)

            def leave_psum(layer, u):
                kind, n = MIXER_UNITS[u]
                dve.wait_ge(unit_done.sem, unit_done.by(layer, u + 1))
                if kind in ("dv", "gv", "gk"):
                    if n % 2 == 1:
                        g = n // 2
                        dve.wait_ge(r_ready.sem, r_ready.by(layer, 2))
                        for t in range(TT):
                            src = bank_of((kind, 2 * g + t // 2))[:, t % 2 * 256:t % 2 * 256 + 256]
                            dst, count = {"dv": (vd[:, t, g * 256:g * 256 + 256], v_ready),
                                          "gv": (vg[:, t, g * 256:g * 256 + 256], gv_ready),
                                          "gk": (kg[:, t // 2, t % 2 * 256:t % 2 * 256 + 256], gk_ready)}[kind]
                            nc.vector.tensor_scalar(dst, src, rtok[:, t:t + 1], None, ALU.mult).then_inc(count.sem, 1)
                    return
                dst, count = {"q": (qk[:, 2 * n, :], qk_raw), "k": (qk[:, 2 * n + 1, :], qk_raw),
                              "gq": (gq[:, n % 2, :], gq_ready),
                              "r": (act_lo_f32[:, head_slot(f"g{n}"), :], rg_ready)}[kind]
                dve.wait_ge(r_ready.sem, r_ready.by(layer, 1))
                tt(dst, bank_of((kind, n))[:, :], rbc[:, :], ALU.mult).then_inc(count.sem, 1)

            def maxima(layer, t):
                h, part = STEPS[t]
                blocks = PARTS[part]
                dve.wait_ge(scores_done.sem, scores_done.by(layer, t + 1))
                for i, c0 in blocks:
                    hidden = c0 + i * P + CHUNK
                    last = nc.vector.memset(sc_ps[0:CHUNK, :, hidden:hidden + CHUNK], NEG)
                last.then_inc(masked.sem, 1)
                dve.wait_ge(masked.sem, masked.by(layer, t + 1))
                for b, (i, c0) in enumerate(blocks):
                    last = nc.vector.tensor_reduce(mx[:, t % 2, 2 * b:2 * b + 2], sc_ps[:, :, c0:c0 + (i + 1) * P],
                                                   AX_X, ALU.max)
                last.then_inc(max_done.sem, 1)
                dve.wait_ge(max_done.sem, max_done.by(layer, t + 1))
                n = 2 * len(blocks)
                nc.vector.tensor_scalar(neg_mx[:, t % 2, 0:n], mx[:, t % 2, 0:n], -DH ** -0.5, None, ALU.mult)\
                    .then_inc(neg_max_ready.sem, 1)

            def combine(layer, t):
                h, part = STEPS[t]
                blocks = PARTS[part]
                n = len(blocks)
                dve.wait_ge(probs_ready.sem, probs_ready.by(layer, t + 1))
                nc.vector.reciprocal(p_rec[:, t % 2, 0:2 * n], p_sum[:, t % 2, 0:2 * n]).then_inc(rec_ready.sem, 1)
                dve.wait_ge(rec_ready.sem, rec_ready.by(layer, t + 1))
                odd = p_rec[:, t % 2, 0:2 * n].rearrange("p (b j) -> p b j", j=2)[:, :, 1]
                nc.vector.tensor_scalar(p_lam[:, t % 2, 0:n], odd, neg_lam[:, bass.ds(layer, 1)], None, ALU.mult)\
                    .then_inc(lam_scaled.sem, 1)
                if t >= 2:
                    dve.wait_ge(transposed.sem, transposed.by(layer, t - 1))
                for b, (i, c0) in enumerate(blocks):
                    cols = slice(c0, c0 + (i + 1) * P)
                    last = nc.vector.tensor_scalar(a_buf[:, t % 2, cols], probs[:, 0, cols],
                                                   p_rec[:, t % 2, 2 * b:2 * b + 1], None, ALU.mult)
                last.then_inc(a_half.sem, 1)
                dve.wait_ge(lam_scaled.sem, lam_scaled.by(layer, t + 1))
                dve.wait_ge(a_half.sem, a_half.by(layer, t + 1))
                for b, (i, c0) in enumerate(blocks):
                    cols = slice(c0, c0 + (i + 1) * P)
                    last = stt(a_buf[:, t % 2, cols], probs[:, 1, cols], p_lam[:, t % 2, b:b + 1],
                               a_buf[:, t % 2, cols], ALU.mult, ALU.add)
                last.then_inc(a_ready.sem, 1)

            def apply_norm(layer, e):
                name = SUMS[e][0]
                h = int(name[1])
                if name[0] in "qk":
                    t, g, count = (qk[:, 2 * h + (name[0] == "k"), :],
                                   qk_g[:, bass.ds(layer + (0 if name[0] == "q" else L), 1)], qk_scaled)
                elif name[0] == "d":
                    t, g, count = act_lo_f32[:, head_slot(name), :], sub_g[:, bass.ds(layer, 1)], o_normed
                else:
                    t, g, count = act_hi_f32[:, head_slot(name), :], params[:, bass.ds(layer + C_GG, 1)], o_normed
                dve.wait_ge(rs_ready.sem, rs_ready.by(layer, e + 1))
                stt(t, t, g, rs[:, e % 2, :], ALU.mult, ALU.mult).then_inc(count.sem, 1)

            def newton_step(layer, e):
                k = qk_sums.index(e) + 1
                name = SUMS[e][0]
                t = qk[:, 2 * int(name[1]) + (name[0] == "k"), :]
                dve.wait_ge(rs_squared.sem, rs_squared.by(layer, k))
                step = newton[:, (k - 1) % 2, :]
                stt(step, bank_of(("sum", e))[:, :], DH * EPS, step, ALU.add, ALU.mult)\
                    .then_inc(newton_product.sem, 1)
                dve.wait_ge(newton_product.sem, newton_product.by(layer, k))
                dve.wait_ge(qk_scaled.sem, qk_scaled.by(layer, k))
                stt(t, step, -3.0 * DH, t, ALU.add, ALU.mult).then_inc(qk_ready.sem, 1)

            def qk_to_lo(layer, k):
                dve.wait_ge(qk_hi_ready.sem, qk_hi_ready.by(layer, k + 1))
                tt(qk_lo[:, k, :], qk[:, k, :], qk_hi(k // 2, k % 2).bitcast(F32), ALU.subtract)\
                    .then_inc(qk_lo_ready.sem, 1)

            def log_gates(layer, p):
                dve.wait_ge(z_log.sem, z_log.by(layer, p + 1))
                stt(la[:, p, :], bank_of(("z", p))[:, :], 0.0, gate_tmp[:, p, :], ALU.min, ALU.subtract)\
                    .then_inc(la_ready.sem, 1)

            def decay_keys(layer, p):
                dve.wait_ge(kd_ready.sem, kd_ready.by(layer, p + 1))
                dve.wait_ge(gk_ready.sem, gk_ready.by(layer, TT))
                tt(kg[:, p, :], kg[:, p, :], kd_tmp[:, p, :], ALU.mult).then_inc(k_decayed.sem, 1)

            def next_state(layer, c):
                dve.wait_ge(kv_done.sem, kv_done.by(layer, c + 1))
                kv = bank_of(("kv", c))[:, :].rearrange("p (a n) -> p a n", a=2)
                if c == 0:
                    for r in range(2):
                        last = nc.vector.tensor_copy(state[r * DK:(r + 1) * DK, 0, :, :],
                                                     kv[r * DK:(r + 1) * DK, :, r * DV:(r + 1) * DV])
                else:
                    dve.wait_ge(decay_ready.sem, decay_ready.by(layer, 1))
                    dve.wait_ge(state_ready.sem, state_ready.by(layer, c))
                    for r in range(2):
                        rows = slice(r * DK, (r + 1) * DK)
                        for a in range(2):
                            last = stt(state[rows, c, a, :], state[rows, c - 1, a, :], decay[rows, a, c:c + 1],
                                       kv[rows, a, r * DV:(r + 1) * DV], ALU.mult, ALU.add)
                last.then_inc(state_ready.sem, 1)

            def gate_head(layer, h):
                slot = head_slot(f"g{h}")
                dve.wait_ge(silu_done.sem, silu_done.by(layer, h + 1))
                dve.wait_ge(o_normed.sem, o_normed.by(layer, RS_USED[SUM_OF[f"g{h}"]][1]))
                tt(act_lo_f32[:, slot, :], act_lo_f32[:, slot, :], act_hi_f32[:, slot, :], ALU.mult)\
                    .then_inc(gated.sem, 1)

            def head_lo(layer, name):
                slot = head_slot(name)
                dve.wait_ge(o_hi_ready.sem, o_hi_ready.by(layer, OUT_ORDER.index(name) + 1))
                tt(act_lo[:, slot, :], act_lo_f32[:, slot, :], act_hi[:, slot, :].bitcast(F32), ALU.subtract)\
                    .then_inc(o_lo_ready.sem, 1)

            with dve.Fori(0, L) as layer:
                prepare_layer(layer)
                for place in range(PLACES):
                    items = small_items(place)
                    if place % 2 == 1:
                        leave_psum(layer, place // 2)
                    for e in qk_sums:
                        if SUMS[e][1] == place - 1:
                            apply_norm(layer, e)
                            newton_step(layer, e)
                    for kind, n in items:
                        if kind == "scores":
                            maxima(layer, n)
                        elif kind == "kv":
                            next_state(layer, n)
                    for kind, n in items:
                        if kind == "sum" and n in o_sums:
                            apply_norm(layer, n)
                    for k, e in enumerate(qk_sums):
                        if SUMS[e][1] == place - 1:
                            qk_to_lo(layer, k)
                    if place > 0:
                        for kind, n in small_items(place - 1):
                            if kind == "scores":
                                combine(layer, n)
                    for kind, n in items:
                        if kind == "low":
                            dve.wait_ge(low_done.sem, low_done.by(layer, 1))
                            dve.wait_ge(layer_ready.sem, layer_ready.by(layer, 4))
                            tt(low_t[0:2 * RANK, :], bank_of(("low", 0))[0:2 * RANK, :], rbc[0:2 * RANK, :], ALU.mult)\
                                .then_inc(low_ready.sem, 1)
                        elif kind == "z":
                            log_gates(layer, n)
                        elif kind == "suf":
                            decay_keys(layer, n)
                    if place == end(23):
                        gate_head(layer, 2)
                    if place in HEAD_SPLIT:
                        head_lo(layer, HEAD_SPLIT[place])
                    if place == mid(22):
                        gate_head(layer, 0)
                        gate_head(layer, 1)
                    if place == end(22):
                        head_lo(layer, "g0")
                        head_lo(layer, "g1")
                gate_head(layer, 3)
                head_lo(layer, "g2")
                head_lo(layer, "g3")

                dve.wait_ge(act_moved, layer * (16 * KT) + CONSTS_LANDED)
                dve.wait_ge(tokens_summed.sem, tokens_summed.by(layer, 2))
                nc.vector.memset(acc[:, :], 0.0).then_inc(acc_zeroed.sem, 1)
                with dve.Fori(0, KT // SLOTS) as i:
                    for s in range(SLOTS):
                        m = i * SLOTS + s
                        dve.wait_ge(unit_done.sem, unit_done.by(layer, i * SLOTS + (U_OUT + s + 1)))
                        tt(x[:, m, :], x[:, m, :], bank[ROUND[s]][:, :], ALU.add).then_inc(x_ready.sem, 1)
                        dve.wait_ge(x_ready.sem, x_ready.by(layer, m + 1))
                        normed_lo(layer, m + KT, m, layer * KT + i * SLOTS + (C_N2 + s))

                nc.vector.memset(u_buf[:, :, 0:2], 0.0).then_inc(pads_zeroed.sem, 1)
                dve.wait_ge(pads_zeroed.sem, pads_zeroed.by(layer, 1))
                dve.wait_ge(r_ready.sem, r_ready.by(layer, 3))

                def conv_col(tap, i, s):
                    return layer * (4 * 2 * FT) + i * 2 + (C_CONV + tap * 2 * FT + s // 2 + (s % 2) * FT)

                def convolve(i, s):
                    n = i * SLOTS + s
                    dve.wait_ge(tap2_done.sem, tap2_done.by(layer, n + 1))
                    stt(c_buf[:, s, :], u_buf[:, s, 1:T + 1], params[:, bass.ds(conv_col(1, i, s), 1)], c_buf[:, s, :],
                        ALU.mult, ALU.add).then_inc(tap1_done.sem, 1)
                    dve.wait_ge(tap1_done.sem, tap1_done.by(layer, n + 1))
                    stt(c_buf[:, s, :], u_buf[:, s, 0:T], params[:, bass.ds(conv_col(0, i, s), 1)], c_buf[:, s, :],
                        ALU.mult, ALU.add).then_inc(conv_done.sem, 1)

                def product(j, n, s):
                    dve.wait_ge(gate_ready.sem, gate_ready.by(layer, j + 1))
                    dve.wait_ge(conv_done.sem, conv_done.by(layer, n + 1))
                    tt(c_buf[:, s, :], c_buf[:, s, :], c_buf[:, s - 1, :], ALU.mult).then_inc(product_ready.sem, 1)

                def lo_of_product(j, s):
                    dve.wait_ge(act_hi_ready.sem, act_hi_ready.by(layer, j + 1))
                    tt(act_lo[:, j, :], c_buf[:, s, :], act_hi[:, j, :].bitcast(F32), ALU.subtract)\
                        .then_inc(act_lo_ready.sem, 1)

                def up_stage(i, s, first):
                    n = i * SLOTS + s
                    dve.wait_ge(unit_done.sem, unit_done.by(layer, n + (U_UP + 1)))
                    tt(u_buf[:, s, 2:T + 2], bank[ROUND[s]][:, :], rbc[:, :], ALU.mult).then_inc(u_ready.sem, 1)
                    if s == 3:
                        lo_of_product(i * 2, 1)
                    if s == 1 and not first:
                        lo_of_product(i * 2 - 1, 3)
                    if s > 0:
                        convolve(i, s - 1)
                    elif not first:
                        convolve(i - 1, 3)
                    if s == 2:
                        product(i * 2, n - 1, 1)
                    if s == 0 and not first:
                        product(i * 2 - 1, n - 1, 3)

                for s in range(SLOTS):
                    up_stage(0, s, True)
                with dve.Fori(1, 2 * FT // SLOTS) as i:
                    for s in range(SLOTS):
                        up_stage(i, s, False)
                convolve(2 * FT // SLOTS - 1, 3)
                product(FT - 1, 2 * FT - 1, 3)
                lo_of_product(FT - 1, 3)

                dve.wait_ge(tokens_summed.sem, tokens_summed.by(layer, 3))
                nc.vector.memset(acc[:, :], 0.0).then_inc(acc_zeroed.sem, 1)
                with dve.Fori(0, KT // SLOTS) as i:
                    for s in range(SLOTS):
                        m = i * SLOTS + s
                        dve.wait_ge(unit_done.sem, unit_done.by(layer, i * (3 * SLOTS) + (U_DOWN + 3 * (s + 1))))
                        tt(x[:, m, :], x[:, m, :], bank[DOWN_ROUND[s]][:, :], ALU.add).then_inc(x_ready.sem, 1)
                        dve.wait_ge(x_ready.sem, x_ready.by(layer, m + KT + 1))
                        normed_lo(layer, m + 2 * KT, m, layer * KT + i * SLOTS + (C_N1 + KT + s))

        @block.tensor
        def _(pe):
            def mm(out_, lhsT, rhs, start, stop, **kw):
                return nc.tensor.matmul(out_, lhsT, rhs, start=start, stop=stop, **kw)

            def three(out_, hi, lo, rhs_hi, rhs_lo, start, stop, **kw):
                mm(out_, hi, rhs_hi, start, False, **kw)
                mm(out_, lo, rhs_hi, False, False, **kw)
                return mm(out_, hi, rhs_lo, False, stop, **kw)

            def weights(s, k):
                return w_hi[:, s, k * P:(k + 1) * P], w_lo[:, s, k * P:(k + 1) * P]

            def rows_tile(layer, u):
                kind, n = MIXER_UNITS[u]
                s = u % SLOTS
                pe.wait_ge(lo_ready.sem, lo_ready.by(layer, u + 1))
                b = take_bank(layer, (kind, n))
                for k in range(KT):
                    if k == MID_TILE:
                        at_place(layer, mid(u))
                    last = three(b[:, :], *weights(s, k), h_hi[:, k, :], h_lo[:, k, :], k == 0, k == KT - 1)
                last.then_inc(unit_done.sem, 1)

            def token_tiles(layer, u):
                kind, n = MIXER_UNITS[u]
                s = u % SLOTS
                pe.wait_ge(lo_ready.sem, lo_ready.by(layer, u + 1))
                if n % 2 == 0:
                    take_two(layer, (kind, n))
                g = n // 2
                for kk in range(KT // 2):
                    k = n % 2 * (KT // 2) + kk
                    if kk == KT // 4:
                        at_place(layer, mid(u))
                    if u == 0 and kk > 0:
                        pe.wait_ge(first_lo_quarters, kk)
                    if u < 2:
                        pe.wait_ge(h_lo_ready.sem, h_lo_ready.by(layer, k + 1))
                    whi, wlo = (w[:, s, kk * 256:(kk + 1) * 256] for w in (w_hi, w_lo))
                    for t in range(TT):
                        o = bank_of((kind, 2 * g + t // 2))[:, t % 2 * 256:t % 2 * 256 + 256]
                        tok = slice(t * P, (t + 1) * P)
                        first, end = k == 0 and t % 2 == 0, k == KT - 1
                        mm(o, h_hi[:, k, tok], whi, first, False, skip_group_check=True)
                        mm(o, h_hi[:, k, tok], wlo, False, False, skip_group_check=True)
                        last = mm(o, h_lo[:, k, tok], whi, False, end, skip_group_check=True)
                last.then_inc(unit_done.sem, 1)

            def sum_tokens(layer, added):
                pe.wait_ge(acc_added.sem, acc_added.by(layer, added))
                mm(o_ps[:, :], ones, acc[:, :], True, True).then_inc(tokens_summed.sem, 1)

            def scores(layer, t):
                h, part = STEPS[t]
                pe.wait_ge(qk_lo_ready.sem, qk_lo_ready.by(layer, 2 * h + 2))
                if t == 0:
                    pe.wait_ge(ln_tokens.sem, ln_tokens.by(layer, 2))
                else:
                    pe.wait_ge(probs_ready.sem, probs_ready.by(layer, t))
                for i, c0 in PARTS[part]:
                    for j in range(2):
                        rows = slice(j * DH, (j + 1) * DH)
                        queries, keys = slice(i * P, (i + 1) * P), slice(0, (i + 1) * P)
                        last = three(sc_ps[:, j, c0:c0 + (i + 1) * P],
                                     qk_hi(h, 0)[rows, queries], qk_lo[rows, 2 * h, queries],
                                     qk_hi(h, 1)[rows, keys], qk_lo[rows, 2 * h + 1, keys], True, True)
                last.then_inc(scores_done.sem, 1)

            def transposes(layer, t):
                pe.wait_ge(a_ready.sem, a_ready.by(layer, t + 1))
                if t > 0:
                    pe.wait_ge(aT_ready.sem, aT_ready.by(layer, t))
                else:
                    pe.wait_ge(lam_exp_ready, 1)
                n = 0
                for i, c0 in PARTS[STEPS[t][1]]:
                    for j in range(i + 1):
                        last = nc.tensor.transpose(t_ps[:, n * P:(n + 1) * P],
                                                   a_buf[:, t % 2, c0 + j * P:c0 + (j + 1) * P], ident)
                        n += 1
                last.then_inc(transposed.sem, 1)

            def values(layer, t):
                h, part = STEPS[t]
                pe.wait_ge(aT_ready.sem, aT_ready.by(layer, t + 1))
                pe.wait_ge(v_ready.sem, v_ready.by(layer, 2 * TT))
                if part == 0:
                    if h == 0:
                        pe.wait_ge(ln_tokens.sem, ln_tokens.by(layer, 1))
                    else:
                        pe.wait_ge(o_copied.sem, o_copied.by(layer, RS_USED[SUM_OF[f"d{h - 1}"]][1]))
                n = 0
                for i, _ in PARTS[part]:
                    for j in range(i + 1):
                        last = mm(o_ps[:, i * P:(i + 1) * P], vd[:, j, h * DV:(h + 1) * DV],
                                  aT[:, t % 2, n * P:(n + 1) * P], j == 0, j == i)
                        n += 1
                last.then_inc(pv_done.sem, 1)

            def small(layer, kind, n):
                if kind == "ss":
                    sum_tokens(layer, KT)
                elif kind == "rtok":
                    for t in range(TT):
                        last = mm(sc_ps[:, 0, t:t + 1], acc[:, t * P:(t + 1) * P], ones[:, 0:1], True, True)
                    last.then_inc(tokens_summed.sem, 1)
                elif kind == "T":
                    transposes(layer, n)
                elif kind == "values":
                    values(layer, n)
                elif kind == "scores":
                    scores(layer, n)
                elif kind == "sum":
                    b = take_bank(layer, ("sum", n))
                    if n == 0:
                        pe.wait_ge(map_ready, 1)
                    pe.wait_ge(squares_split.sem, squares_split.by(layer, n + 1))
                    m = same_map_r if SUMS[n][0][0] in "qk" else ones_r
                    mm(b[:, :], m[:, :], sq_hi[:, n % 2, :], True, False)
                    mm(b[:, :], m[:, :], sq_lo[:, n % 2, :], False, True).then_inc(summed.sem, 1)
                elif kind == "low":
                    b = take_bank(layer, ("low", 0))
                    pe.wait_ge(layer_ready.sem, layer_ready.by(layer, 4))
                    for k in range(KT):
                        pair = act_lo[:, 6, 2 * k * RANK:2 * (k + 1) * RANK]
                        mm(b[0:2 * RANK, :], pair, h_hi[:, k, :], k == 0, False, skip_group_check=True)
                        last = mm(b[0:RANK, :], pair[:, 0:RANK], h_lo[:, k, :], False, k == KT - 1, skip_group_check=True)
                    last.then_inc(low_done.sem, 1)
                elif kind == "z":
                    b = take_bank(layer, ("z", n))
                    pe.wait_ge(low_ready.sem, low_ready.by(layer, 1))
                    for t in range(2):
                        tok = (2 * n + t) * P
                        last = mm(b[:, t * 256:(t + 1) * 256], low_t[:, tok:tok + P], gk_up_now, True, True)
                    last.then_inc(z_done.sem, 1)
                elif kind == "suf":
                    b = take_bank(layer, ("suf", n))
                    pe.wait_ge(la_ready.sem, la_ready.by(layer, n + 1))
                    mm(b[:, :], later, la[:, n, :], True, True).then_inc(suffix_done.sem, 1)
                elif kind == "dec":
                    b = take_bank(layer, ("dec", n))
                    pe.wait_ge(la_ready.sem, la_ready.by(layer, 2))
                    for p in range(2):
                        for t in range(TT):
                            c0 = t % 2 * 256 + p * P
                            last = mm(b[:, p * NC + 2 * t:p * NC + 2 * t + 2], la[:, t // 2, c0:c0 + P], halves,
                                      True, True)
                    last.then_inc(decay_done.sem, 1)
                elif kind == "kv":
                    b = take_bank(layer, ("kv", n))
                    pe.wait_ge(k_decayed.sem, k_decayed.by(layer, 2))
                    pe.wait_ge(gv_ready.sem, gv_ready.by(layer, 2 * TT))
                    t, rows = n // 2, slice(n % 2 * CHUNK, (n % 2 + 1) * CHUNK)
                    for a in range(2):
                        c0 = t % 2 * 256 + a * P
                        last = mm(b[:, a * 256:(a + 1) * 256], kg[rows, t // 2, c0:c0 + P],
                                  vg[rows, t, a * 256:(a + 1) * 256], True, True)
                    last.then_inc(kv_done.sem, 1)
                elif kind == "go":
                    b = take_bank(layer, ("go", n))
                    pe.wait_ge(state_ready.sem, state_ready.by(layer, NC))
                    pe.wait_ge(gq_ready.sem, gq_ready.by(layer, n // 2 + 1))
                    rows = slice(n % 2 * DK, (n % 2 + 1) * DK)
                    for c in range(NC):
                        cols = slice(c * CHUNK, (c + 1) * CHUNK)
                        last = mm(b[:, cols], state[rows, c, n // 2, :], gq[rows, n // 2, cols], True, True)
                    last.then_inc(go_done.sem, 1)

            def at_place(layer, place):
                for kind, n in small_items(place):
                    small(layer, kind, n)

            pe.wait_ge(lam_prod_ready, 1)
            pe.wait_ge(ones_ready, 1)
            mm(t_ps[:, 0:2 * L], ones, lam_prod[:, :], True, True).then_inc(lam_summed, 1)

            with pe.Fori(0, L) as layer:
                for u in range(U_OUT):
                    if MIXER_UNITS[u][0] in ("dv", "gk", "gv"):
                        token_tiles(layer, u)
                    else:
                        rows_tile(layer, u)
                    at_place(layer, end(u))

                with pe.Fori(0, KT // SLOTS) as i:
                    for s in range(SLOTS):
                        pe.wait_ge(lo_ready.sem, lo_ready.by(layer, i * SLOTS + (U_OUT + s + 1)))
                        mixers_use, k = given_back(LAST_IN[ROUND[s]])
                        pe.wait_ge(mixers_use.sem, mixers_use.by(layer, k))
                        pe.wait_ge(h_lo_ready.sem, h_lo_ready.by(layer, i * SLOTS + (KT - SLOTS + s + 1)))
                        for j, name in enumerate(OUT_ORDER):
                            k = head_slot(name)
                            if s == 0:
                                pe.wait_ge(o_lo_ready.sem, o_lo_ready.by(layer, j + 1))
                            last = three(bank[ROUND[s]][:, :], *weights(s, k), act_hi[:, k, :], act_lo[:, k, :],
                                         j == 0, j == KT - 1)
                        last.then_inc(unit_done.sem, 1)

                def up_unit(i, s, first):
                    pe.wait_ge(lo_ready.sem, lo_ready.by(layer, i * SLOTS + (U_UP + s + 1)))
                    free = 2 * KT - SLOTS + s + 1
                    if not first:
                        pe.wait_ge(u_ready.sem, u_ready.by(layer, i * SLOTS + (s - SLOTS + 1)))
                    for k in range(KT):
                        if first and s == 0:
                            pe.wait_ge(h_lo_ready.sem, h_lo_ready.by(layer, max(KT + k + 1, free)))
                        last = three(bank[ROUND[s]][:, :], *weights(s, k), h_hi[:, k, :], h_lo[:, k, :], k == 0, k == KT - 1)
                    last.then_inc(unit_done.sem, 1)

                for s in range(SLOTS):
                    up_unit(0, s, True)
                    if s == 0:
                        pe.wait_ge(o_copied.sem, o_copied.by(layer, 2 * H))
                        sum_tokens(layer, 2 * KT)
                with pe.Fori(1, 2 * FT // SLOTS) as i:
                    for s in range(SLOTS):
                        up_unit(i, s, False)

                with pe.Fori(0, KT // SLOTS) as i:
                    for s in range(SLOTS):
                        pe.wait_ge(u_ready.sem, u_ready.by(layer, 2 * FT - SLOTS + ROUND.index(DOWN_ROUND[s]) + 1))
                        pe.wait_ge(x_ready.sem, x_ready.by(layer, i * SLOTS + (KT - SLOTS + s + 1)))
                        j = 0
                        for c, blocks in enumerate(DOWN_BLOCKS):
                            slot = (3 * s + c) % SLOTS
                            pe.wait_ge(lo_ready.sem, lo_ready.by(layer, i * (3 * SLOTS) + (U_DOWN + 3 * s + c + 1)))
                            for k in range(blocks):
                                if s == 0:
                                    pe.wait_ge(act_lo_ready.sem, act_lo_ready.by(layer, j + 1))
                                last = three(bank[DOWN_ROUND[s]][:, :], *weights(slot, k), act_hi[:, j, :], act_lo[:, j, :],
                                             j == 0, j == FT - 1)
                                j += 1
                            last.then_inc(unit_done.sem, 1)


def units_of_weights(w_in, w_out, w_up, w_down):
    starts = np.concatenate([[0], np.cumsum(IN_SPLITS)])
    first = dict(zip(("gq", "gk", "gv", "r", "low", "q", "k", "dv"), starts))

    def columns(w, c0):
        return w[:, c0:c0 + P].reshape(-1, P, P).transpose(1, 0, 2).reshape(P, -1)

    units = []
    for layer in range(L):
        for kind, n in MIXER_UNITS:
            c0 = first[kind]
            if kind in ("dv", "gk", "gv"):
                rows = w_in[layer, n % 2 * (D // 2):(n % 2 + 1) * (D // 2), c0 + n // 2 * 256:c0 + n // 2 * 256 + 256]
                units.append(rows.reshape(KT // 2, P, 256).transpose(1, 0, 2).reshape(P, -1))
            else:
                units.append(columns(w_in[layer], c0 + n * P))
        units += [columns(w_out[layer], m * P) for m in range(KT)]
        for j in range(FT):
            units += [columns(w_up[layer], j * P), columns(w_up[layer], FF + j * P)]
        for m in range(KT):
            whole = columns(w_down[layer], m * P)
            k = 0
            for blocks in DOWN_BLOCKS:
                part = whole[:, k * P:(k + blocks) * P]
                units.append(np.pad(part, ((0, 0), (0, 1024 - blocks * P))))
                k += blocks
    units += [np.zeros((P, 1024), np.float32)] * AHEAD
    low = w_in[:, :, first["low"]:first["low"] + RANK].reshape(L, KT, P, RANK).transpose(2, 0, 1, 3).reshape(P, L, -1)
    return np.stack(units), low


def columns_of_params(inputs):
    def tiles(a):
        return a.reshape(-1, P).T

    cols = [tiles(inputs["norm1_g"]), np.zeros((P, KT), np.float32), tiles(inputs["norm2_g"])]
    for layer in range(L):
        cols += [tiles(inputs["ffn_conv_w"][layer]), tiles(inputs["ffn_conv_b"][layer])]
    cols += [tiles(inputs["gla_norm_g"]), tiles(inputs["diff_sub_g"])]
    cols += [np.tile(inputs[k].T, (2, 1)) for k in ("diff_q_norm_g", "diff_k_norm_g")]
    cols += [np.pad(inputs[k].T, ((0, P - DH), (0, 0))) for k in ("diff_lam_q1", "diff_lam_q2", "diff_lam_k1", "diff_lam_k2")]
    return np.concatenate(cols, axis=1)


def constants():
    row, col = np.arange(P)[:, None], np.arange(P)[None, :]
    same = row // CHUNK == col // CHUNK
    init = [0.8 - 0.6 * float(np.exp(-0.3 * layer)) for layer in range(L)]
    cols = [row == col, same, same & (row > col), row // CHUNK == np.arange(2)[None, :],
            np.full((P, 1), EPS), np.tile([init], (P, 1)), np.tile([[1.0 - v for v in init]], (P, 1))]
    return np.concatenate([np.asarray(c, np.float32) for c in cols], axis=1)


def kernel(**inputs):
    import concourse.bacc as bacc
    from concourse.bass_utils import run_bass_kernel_spmd

    inputs = {k: np.asarray(v) for k, v in inputs.items()}
    units, low = units_of_weights(inputs["w_in"], inputs["w_out"], inputs["ffn_w_up"], inputs["ffn_w_down"])
    gk_up = np.concatenate([inputs["gla_w_gk_up"], inputs["gla_w_gk_up"], inputs["gla_b_gk"][:, None, :]], axis=1).transpose(1, 0, 2)
    arrays = {
        "in_x": inputs["x"][0].T.reshape(KT, P, T).transpose(1, 0, 2), "in_units": units, "in_low": low, "in_gk_up": gk_up,
        "in_params": columns_of_params(inputs), "in_consts": constants(),
    }
    arrays = {k: np.ascontiguousarray(v) for k, v in arrays.items()}
    nc = bacc.Bacc("TRN2", target_bir_lowering=False, num_devices=1)
    args = [nc.dram_tensor(k, v.shape, mybir.dt.from_np(v.dtype), kind="ExternalInput").ap() for k, v in arrays.items()]
    args.append(nc.dram_tensor("out_x", (KT, P, T), F32, kind="ExternalOutput").ap())
    trunk(nc, *args)
    r = run_bass_kernel_spmd(nc, [arrays], core_ids=[0])
    return r.results[0]["out_x"].reshape(D, T).T.reshape(1, T, D)
```
